# Optimizing a Trainium2 kernel written in Bass

```python
import jax, jax.numpy as jnp
from jax import lax
import numpy as np

D_MODEL = 1024
BATCH = 1
SEQ = 1024
DEPTH = 1
DEC_BATCH = 1
DEC_SEQ = 32
PAST_LEN = 128

CHUNK = 64
D_MIX = D_MODEL
HEAD_DIM = 64
ATTN_WIDTH = D_MIX // 2
N_HEADS = ATTN_WIDTH // HEAD_DIM
N_KV_HEADS = 2
GQA_REP = N_HEADS // N_KV_HEADS
WINDOW = 128
WIN_CHUNKS = WINDOW // CHUNK
WIN_KEEP = WINDOW
ATTN_SCALE = HEAD_DIM ** -0.5
NEG_BIG = -1e30
GMLP_WIDTH = D_MIX - ATTN_WIDTH
GMLP_CHUNK = 128
GMLP_GROUPS = 4
GMLP_GROUP_DIM = GMLP_WIDTH // GMLP_GROUPS
Q_COLS = N_HEADS * HEAD_DIM
KV_COLS = N_KV_HEADS * HEAD_DIM
IN_COLS = Q_COLS + 2 * KV_COLS + 2 * GMLP_WIDTH
SPLITS = (Q_COLS, Q_COLS + KV_COLS, Q_COLS + 2 * KV_COLS, Q_COLS + 2 * KV_COLS + GMLP_WIDTH)
D_FF = -(-8 * D_MODEL // (3 * 256)) * 256

kernel_name = "hybrid_swa_sink_gmlp_streaming_step"

def rms_norm(x, g, eps=1e-6):
    xf = x.astype(jnp.float32)
    y = xf * lax.rsqrt(jnp.mean(xf * xf, axis=-1, keepdims=True) + eps)
    return (y * g.astype(jnp.float32)).astype(x.dtype)

def group_layer_norm(x, g, b, eps=1e-5):
    xs = x.reshape(x.shape[:-1] + (GMLP_GROUPS, GMLP_GROUP_DIM)).astype(jnp.float32)
    mu = jnp.mean(xs, axis=-1, keepdims=True)
    var = jnp.mean(jnp.square(xs - mu), axis=-1, keepdims=True)
    y = (xs - mu) * lax.rsqrt(var + eps)
    y = y * g.reshape(GMLP_GROUPS, GMLP_GROUP_DIM).astype(jnp.float32) + b.reshape(GMLP_GROUPS, GMLP_GROUP_DIM).astype(jnp.float32)
    return y.astype(x.dtype)

def project(h, w_in):
    z = h @ w_in
    q, k, v, u, g = jnp.split(z, SPLITS, axis=-1)
    lead = h.shape[:-1]
    q = q.reshape(lead + (N_KV_HEADS, GQA_REP, HEAD_DIM))
    k = k.reshape(lead + (N_KV_HEADS, HEAD_DIM))
    v = v.reshape(lead + (N_KV_HEADS, HEAD_DIM))
    return q, k, v, u, g

def sink_probs(scores, mask, sinks):
    s = sinks.astype(jnp.float32).reshape(N_KV_HEADS, GQA_REP, 1, 1)
    scores = jnp.where(mask, scores, NEG_BIG)
    m = jnp.maximum(jnp.max(scores, axis=-1, keepdims=True), s)
    p = jnp.exp(scores - m)
    return p / (jnp.sum(p, axis=-1, keepdims=True) + jnp.exp(s - m))

def window_attention_prompt(q, k, v, sinks):
    B, T = q.shape[0], q.shape[1]
    nc = T // CHUNK
    qc = q.reshape(B, nc, CHUNK, N_KV_HEADS, GQA_REP, HEAD_DIM).astype(jnp.float32)
    kc = k.reshape(B, nc, CHUNK, N_KV_HEADS, HEAD_DIM)
    vc = v.reshape(B, nc, CHUNK, N_KV_HEADS, HEAD_DIM)

    def band(x):
        parts = [jnp.pad(x, ((0, 0), (j, 0), (0, 0), (0, 0), (0, 0)))[:, :nc] for j in range(WIN_CHUNKS - 1, -1, -1)]
        return jnp.concatenate(parts, axis=2)

    kb, vb = band(kc), band(vc)
    shift = jnp.repeat(jnp.arange(WIN_CHUNKS - 1, -1, -1), CHUNK)
    valid = jnp.arange(nc)[:, None] >= shift[None, :]
    mask = valid[None, :, None, None, None, :]
    scores = jnp.einsum('bnqkrd,bnskd->bnkrqs', qc, kb.astype(jnp.float32)) * ATTN_SCALE
    probs = sink_probs(scores, mask, sinks)
    out = jnp.einsum('bnkrqs,bnskd->bnqkrd', probs.astype(v.dtype), vb)
    return out.reshape(B, T, ATTN_WIDTH)

def window_attention_sample(q, k, v, cache_k, cache_v, sinks):
    S = q.shape[1]
    keys = jnp.concatenate([cache_k.astype(k.dtype), k], axis=1)
    vals = jnp.concatenate([cache_v.astype(v.dtype), v], axis=1)
    key_pos = jnp.concatenate([PAST_LEN - WIN_KEEP + jnp.arange(WIN_KEEP), PAST_LEN + jnp.arange(S)])
    q_pos = PAST_LEN + jnp.arange(S)
    dchunk = (q_pos // CHUNK)[:, None] - (key_pos // CHUNK)[None, :]
    mask = (dchunk >= 0) & (dchunk < WIN_CHUNKS)
    scores = jnp.einsum('bqkrd,bskd->bkrqs', q.astype(jnp.float32), keys.astype(jnp.float32)) * ATTN_SCALE
    probs = sink_probs(scores, mask, sinks)
    out = jnp.einsum('bkrqs,bskd->bqkrd', probs.astype(vals.dtype), vals)
    return out.reshape(q.shape[0], S, ATTN_WIDTH), keys[:, -WIN_KEEP:], vals[:, -WIN_KEEP:]

def gmlp_prompt(u, g, ln_g, ln_b, w_sp, b_sp):
    B, T = u.shape[0], u.shape[1]
    vn = group_layer_norm(jax.nn.gelu(g, approximate=False), ln_g, ln_b)
    vb = vn.reshape(B, T // GMLP_CHUNK, GMLP_CHUNK, GMLP_GROUPS, GMLP_GROUP_DIM)
    mix = jnp.einsum('gts,bnsgc->bntgc', jnp.tril(w_sp), vb) + b_sp.T[:, :, None]
    gate = mix.reshape(B, T, GMLP_GROUPS, GMLP_GROUP_DIM)
    ua = jax.nn.gelu(u, approximate=False).reshape(B, T, GMLP_GROUPS, GMLP_GROUP_DIM)
    return (ua * gate).reshape(B, T, GMLP_WIDTH)

def gmlp_sample(u, g, ln_g, ln_b, w_sp, b_sp):
    DB, S = u.shape[0], u.shape[1]
    vn = group_layer_norm(jax.nn.gelu(g, approximate=False), ln_g, ln_b)
    mix = jnp.einsum('gts,bsgc->btgc', jnp.tril(w_sp)[:, :S, :S], vn) + b_sp.T[:S, :, None]
    ua = jax.nn.gelu(u, approximate=False).reshape(DB, S, GMLP_GROUPS, GMLP_GROUP_DIM)
    return (ua * mix).reshape(DB, S, GMLP_WIDTH), vn.reshape(DB, S, GMLP_WIDTH)

def swiglu(h, w_gate, w_up, w_down):
    return (jax.nn.silu(h @ w_gate) * (h @ w_up)) @ w_down

def setup_inputs(seed: int = 0) -> dict:
    key = jax.random.key(seed)
    ks = jax.random.split(key, 20)
    f32 = jnp.float32
    nrm = lambda k, shape, s: (jax.random.normal(k, shape, f32) * s)
    return {
        "x_prompt": nrm(ks[0], (BATCH, SEQ, D_MODEL), 1.0),
        "x_sample": nrm(ks[1], (DEC_BATCH, DEC_SEQ, D_MODEL), 1.0),
        "cache_attn_k": nrm(ks[2], (DEPTH, DEC_BATCH, WIN_KEEP, N_KV_HEADS, HEAD_DIM), 1.0),
        "cache_attn_v": nrm(ks[3], (DEPTH, DEC_BATCH, WIN_KEEP, N_KV_HEADS, HEAD_DIM), 1.0),
        "g_mix": 1.0 + nrm(ks[4], (DEPTH, D_MODEL), 0.05),
        "w_in": nrm(ks[5], (DEPTH, D_MODEL, IN_COLS), D_MODEL ** -0.5),
        "attn_sinks": nrm(ks[6], (DEPTH, N_HEADS), 0.5),
        "gmlp_ln_g": 1.0 + nrm(ks[7], (DEPTH, GMLP_WIDTH), 0.05),
        "gmlp_ln_b": nrm(ks[8], (DEPTH, GMLP_WIDTH), 0.02),
        "gmlp_w_spatial": nrm(ks[9], (DEPTH, GMLP_GROUPS, GMLP_CHUNK, GMLP_CHUNK), GMLP_CHUNK ** -0.5),
        "gmlp_b_spatial": 1.0 + nrm(ks[10], (DEPTH, GMLP_GROUPS, GMLP_CHUNK), 0.1),
        "w_out": nrm(ks[11], (DEPTH, D_MIX, D_MODEL), D_MIX ** -0.5),
        "g_ffn": 1.0 + nrm(ks[12], (DEPTH, D_MODEL), 0.05),
        "w_gate": nrm(ks[13], (DEPTH, D_MODEL, D_FF), D_MODEL ** -0.5),
        "w_up": nrm(ks[14], (DEPTH, D_MODEL, D_FF), D_MODEL ** -0.5),
        "w_down": nrm(ks[15], (DEPTH, D_FF, D_MODEL), D_FF ** -0.5),
        "g_final": 1.0 + nrm(ks[16], (D_MODEL,), 0.05),
    }

def reference(x_prompt, x_sample, cache_attn_k, cache_attn_v, g_mix, w_in, attn_sinks, gmlp_ln_g, gmlp_ln_b,
              gmlp_w_spatial, gmlp_b_spatial, w_out, g_ffn, w_gate, w_up, w_down, g_final):
    yp, ys = x_prompt, x_sample
    kp_list, vp_list, ks_list, vs_list, gs_list = [], [], [], [], []
    for l in range(DEPTH):
        hp = rms_norm(yp, g_mix[l])
        q, k, v, u, g = project(hp, w_in[l])
        a = window_attention_prompt(q, k, v, attn_sinks[l])
        m = gmlp_prompt(u, g, gmlp_ln_g[l], gmlp_ln_b[l], gmlp_w_spatial[l], gmlp_b_spatial[l])
        yp = yp + jnp.concatenate([a, m], axis=-1) @ w_out[l]
        kp_list.append(k[:, -WIN_KEEP:])
        vp_list.append(v[:, -WIN_KEEP:])

        hs = rms_norm(ys, g_mix[l])
        q, k, v, u, g = project(hs, w_in[l])
        a, k_buf, v_buf = window_attention_sample(q, k, v, cache_attn_k[l], cache_attn_v[l], attn_sinks[l])
        m, g_rows = gmlp_sample(u, g, gmlp_ln_g[l], gmlp_ln_b[l], gmlp_w_spatial[l], gmlp_b_spatial[l])
        ys = ys + jnp.concatenate([a, m], axis=-1) @ w_out[l]
        ks_list.append(k_buf)
        vs_list.append(v_buf)
        gs_list.append(g_rows)

        yp = yp + swiglu(rms_norm(yp, g_ffn[l]), w_gate[l], w_up[l], w_down[l])
        ys = ys + swiglu(rms_norm(ys, g_ffn[l]), w_gate[l], w_up[l], w_down[l])

    y_prompt = rms_norm(yp, g_final)
    y_sample = rms_norm(ys, g_final)
    state_attn_k_prompt = jnp.stack(kp_list)
    state_attn_v_prompt = jnp.stack(vp_list)
    state_attn_k_sample = jnp.stack(ks_list)
    state_attn_v_sample = jnp.stack(vs_list)
    state_gmlp_v_sample = jnp.stack(gs_list)
    return (y_prompt, y_sample, state_attn_k_prompt, state_attn_v_prompt, state_attn_k_sample, state_attn_v_sample, state_gmlp_v_sample)


_drawn_inputs = setup_inputs


def setup_inputs(seed=0):
    import zlib

    import numpy as np

    out = dict(_drawn_inputs(seed))
    spreads = {}
    factors = {'attn_sinks': 8.0, 'gmlp_ln_b': 2.955}
    for name, (base, spread) in spreads.items():
        noise = np.random.default_rng([zlib.crc32(name.encode()), seed]).standard_normal(out[name].shape)
        drawn = base * np.exp(spread * noise) if base else spread * noise
        out[name] = __import__('jax').numpy.asarray(drawn.astype(out[name].dtype))
    for name, factor in factors.items():
        out[name] = (out[name] * factor).astype(out[name].dtype)
    return out
```

```python
from contextlib import ExitStack

import concourse.bass as bass
from concourse import mybir

F32 = mybir.dt.float32
F32R = mybir.dt.float32r
ALU = mybir.AluOpType
ACT = mybir.ActivationFunctionType
AX_X = mybir.AxisListType.X

P = 128
D = 1024
SEQ, DEC = 1024, 32
TOK = SEQ + DEC
ROWS = SEQ // P + 1
SAMPLE = ROWS - 1
BLOCKS = 3
BLK = TOK // BLOCKS
KT = D // P
DH = 64
N_HEADS = 8
PAIRS = 4
GROUPS = 4
Q0, K0, V0, U0, G0 = 0, 512, 640, 768, 1280
SCALE = DH ** -0.5
NEG_BIG = -1e30
D_FF = 2816
CHUNKS = D_FF // (2 * P)
STEPS = 2 * BLOCKS

PROJ = [("v", 0), ("g", 0), ("g", 1), ("g", 2), ("g", 3), ("u", 0), ("u", 1), ("u", 2),
        ("k", 0), ("q", 0), ("q", 1), ("q", 2), ("q", 3), ("u", 3)]
PROJ_BLOCKS = [(0, 0), (1, 0), (0, 1), (1, 1), (0, 2), (1, 2)] + [
    (t, b) for t in range(2, len(PROJ)) for b in range(BLOCKS)]
N_PROJ = len(PROJ)
N_BLOCKS = len(PROJ_BLOCKS)
ATTN_BLOCK = PROJ_BLOCKS.index((PROJ.index(("q", 1)), 0))


def proj_bank(n):
    return n % 4 if n < ATTN_BLOCK else n % 2


def bank_blocks_before(n):
    return n - 3 if n < ATTN_BLOCK else n - 1


STAGE = 3
UNIT_WOUT = N_PROJ
UNIT_FFN = UNIT_WOUT + KT
UNIT_CHUNK = UNIT_FFN + 2

UNITS = 5 * PAIRS


def last_block(t):
    return max(n for n, (tt, _) in enumerate(PROJ_BLOCKS) if tt == t) + 1


def make_schedule():
    s = [("front", 0), ("front", 1), ("back", 0), ("front", 2), ("split", 0), ("back", 1),
         ("front", 3), ("back", 2), ("block", 0, None), ("split", 1), ("front", 4), ("back", 3),
         ("block", 1, None), ("front", 5), ("back", 4), ("front", 6), ("back", 5), ("evac", 0),
         ("block", 2, None), ("front", 7), ("back", 6), ("evac", 1), ("block", 3, None),
         ("front", 8), ("back", 7), ("back", 8), ("evac", 2), ("block", 4, None), ("evac", 3),
         ("block", 5, None), ("evac", 4), ("split", 2), ("evac", 5), ("split", 3)]
    turn = {("v", 0): 6, ("k", 0): 28}
    turn.update({("g", g): 3 * g + 7 for g in range(GROUPS)})
    for n in range(6, N_BLOCKS):
        t, b = PROJ_BLOCKS[n]
        if n == 6:
            s.append(("block", n, None))
            s.append(("consts",))
        elif t >= 10:
            j = t - 10
            s.append(("block", n, 0))
            s.append(("tick", 5 * j + 2 * b))
            s.append(("block", n, 1))
        else:
            s.append(("block", n, None))
        for what, at in turn.items():
            if at == n:
                s.append(("turn",) + what)
        s.append(("evac", n))
        if t >= 10 and b < 2:
            s.append(("tick", 5 * (t - 10) + 2 * b + 1))
        for g in range(GROUPS):
            if n == 3 * g + 8:
                s.append(("affine", g))
            if n == 3 * g + 11:
                s.append(("mix", g))
        if b == BLOCKS - 1 and t + 2 < N_PROJ:
            s.append(("split", t + 2))
        extra = {31: 14, 32: 15, 33: 16, 34: 17, 36: 18, 37: 19}
        extra = {36: 14, 37: 15, 38: 16, 39: 17, 40: 18}
        if n in extra:
            s.append(("split", extra[n]))
    s += [("split", 19), ("tick", 20), ("tick", 21), ("split", 20), ("tick", 22), ("split", 21)]
    for i in range(ROWS):
        s.append(("cat", i))
    for i in range(ROWS):
        s.append(("wout", i))
        if i >= 1:
            s.append(("back", ROWS + i - 1))
        s.append(("front", ROWS + i))
        if i == 5:
            s += [("split", UNIT_FFN), ("split", UNIT_FFN + 1)]
    return s


SCHEDULE = make_schedule()


def side_parts(item):
    kind = item[0]
    if kind == "consts":
        return ["tril", "cache"]
    if kind == "turn":
        return [0] if item[1] == "k" else [0, 1, 2]
    if kind == "mix":
        return [0, 1, 2]
    return []


SIDE = {}
for _item in SCHEDULE:
    for _part in side_parts(_item):
        SIDE[_item + (_part,)] = len(SIDE)
N_SIDE = len(SIDE)


def part_rows(sub):
    return [range(0, 4), range(4, 8), range(8, 9)][sub]


def row_parts(i):
    return slice(0, P) if i != SAMPLE else slice(P - DEC, P)


def row_tokens(i):
    return slice(P * i, P * i + (P if i != SAMPLE else DEC))


def row_window(i):
    return slice(P * i, P * i + P) if i != SAMPLE else slice(TOK - P, TOK)


def build(nc, a, o):
    x_rows = [a["x_prompt"][0, P * i:P * i + P, :] for i in range(SAMPLE)] + [a["x_sample"][0]]
    y_rows = [o["y_prompt"][0, P * i:P * i + P, :] for i in range(SAMPLE)] + [o["y_sample"][0]]

    with ExitStack() as ctx:
        def sb(name, shape, dt=F32):
            return ctx.enter_context(nc.sbuf_tensor(name, shape, dt))

        def sem(name):
            return ctx.enter_context(nc.semaphore(name))

        WORK = 15616
        work_at = -(-nc.sbuf_base // 32) * 32
        work = sb("work", [P, WORK])
        gu_a = nc.alloc_sbuf_tensor_at("gate_up_a", [P, 4, D], F32R, offset=work_at + 4 * 2048)
        t_hi = sb("t_hi", [P, KT, TOK], F32R)
        t_lo = sb("t_lo", [P, KT, TOK], F32R)
        wbuf = sb("wbuf", [P, KT * 2 * D], F32R)
        stage = sb("stage", [P, STAGE, D])
        gain = sb("gain", [P, D])
        trans = sb("trans", [P, 2, TOK])
        wsp_t = sb("wsp_t", [P, GROUPS, P])
        bsp = sb("bsp", [P, GROUPS, P])
        ident = sb("ident", [P, P])
        neg_half = sb("neg_half", [P, 9])
        neg_row = sb("neg_row", [1, DH])
        one_row = sb("one_row", [1, DH])
        sumsq = sb("sumsq", [P, 3 * ROWS])
        meansq = sb("meansq", [P, 3 * ROWS])
        rstd = sb("rstd", [P, 3 * ROWS])
        ln_st = sb("ln_st", [P, ROWS, 6])
        ln_mv = sb("ln_mv", [P, ROWS, 2])
        ln_var = sb("ln_var", [P, ROWS])
        ln_rstd = sb("ln_rstd", [P, ROWS])
        sink8 = sb("sink8", [P, N_HEADS])
        sink = sb("sink", [P, PAIRS, 2, 2])
        nsink = sb("nsink", [P, PAIRS, 2, 2])
        smx = sb("smx", [P, 4, 4])
        nmax = sb("nmax", [P, 4, 4])
        sink_in = sb("sink_in", [P, 4, 4])
        sink_exp = sb("sink_exp", [P, 4, 4])
        psums = sb("psums", [P, 4, 4])
        denom = sb("denom", [P, 4, 4])
        rden = sb("rden", [P, 4, 4])

        cat = work[:, 0:8448].rearrange("p (k t) -> p k t", k=8)
        xn = work[:, 0:2048].rearrange("p (s c) -> p s c", s=2)
        xin = work[:, 4224:4224 + 4096].rearrange("p (s c) -> p s c", s=4)
        k_t = work[:, 8448:9504]
        v_nat = work[:, 9504:10528].rearrange("p (i c) -> p i c", i=8)
        v_even = work[:, 10528:11552].rearrange("p (i c) -> p i c", i=8)
        v_sample = work[:, 11552:11680]
        kc_t = work[:, 11680:11744]
        ln_g = work[:, 11872:12384]
        ln_b = work[:, 12384:12896]
        vn = work[:, 13312:15616].rearrange("p (s i c) -> p s i c", s=2, i=ROWS)
        wsp = work[:, 13312:13824].rearrange("p (g s) -> p g s", g=GROUPS)
        kc_nat = work[0:DH, 15488:15616]
        probs = work[:, 11872:13408].rearrange("p (s h c) -> p s h c", s=3, h=4)
        probs_t = work[:, 13408:14432].rearrange("p (s h c) -> p s h c", s=2, h=4)
        k_state = work[:, 14432:14688].rearrange("p (s c) -> p s c", s=2)
        y_slots = work[:, 6400:15616].rearrange("p (s c) -> p s c", s=ROWS)

        def y_row(i):
            return y_slots[row_parts(i), (i + 2) % ROWS, :]

        w_hl = wbuf[:, :].rearrange("p (s h c) -> p s h c", s=KT, h=2)
        act_hi = wbuf[:, 0:2112].rearrange("p (f t) -> p f t", f=2)
        act_lo = wbuf[:, 2112:4224].rearrange("p (f t) -> p f t", f=2)
        w_dn = wbuf[:, 4224:8320].rearrange("p (f h c) -> p f h c", f=2, h=2)
        gu_b = wbuf[:, 8320:12416].rearrange("p (s c) -> p s c", s=4)
        gu = [gu_a[:, :, :], gu_b]
        silu = trans[:, 0, 0:2 * BLK].rearrange("p (s c) -> p s c", s=2)
        hidden = trans[:, 1, 0:2 * BLK].rearrange("p (s c) -> p s c", s=2)

        ps = ctx.enter_context(nc.psum_tensor("ps", [P, 8, 512], F32))

        x_landed = [sem(f"x_landed{i}") for i in range(4)]
        y_landed = [sem(f"y_landed{i}") for i in range(ROWS)]
        stage_landed = [sem(f"stage_landed{i}") for i in range(STAGE)]
        gain_landed = sem("gain_landed")
        wsp_landed = sem("wsp_landed")
        small_landed = sem("small_landed")
        sink_landed = sem("sink_landed")
        cache_landed = sem("cache_landed")
        states_out = sem("states_out")
        v_state_out = sem("v_state_out")
        k_state_out = sem("k_state_out")
        g_state_out = [sem(f"g_state_out{i}") for i in range(2)]
        y_out = [sem(f"y_out{i}") for i in range(2)]
        pool_consts = sem("pool_consts")
        tril_ready = sem("tril_ready")
        sumsq_ready = sem("sumsq_ready")
        meansq_ready = sem("meansq_ready")
        rstd_ready = sem("rstd_ready")
        xn_ready = sem("xn_ready")
        turned = sem("turned")
        hi_ready = sem("hi_ready")
        lo_ready = sem("lo_ready")
        split_hi = sem("split_hi")
        split_lo = sem("split_lo")
        proj_done = sem("proj_done")
        proj_evac = sem("proj_evac")
        side_done = sem("side_done")
        side_freed = sem("side_freed")
        v_even_zero = sem("v_even_zero")
        v_copied = sem("v_copied")
        ln_stats = sem("ln_stats")
        ln_aggr = sem("ln_aggr")
        ln_centred = sem("ln_centred")
        ln_var_ready = sem("ln_var_ready")
        ln_rstd_ready = sem("ln_rstd_ready")
        vn_ready = sem("vn_ready")
        m_ready = sem("m_ready")
        sinks_ready = sem("sinks_ready")
        scores_done = sem("scores_done")
        max_ready = sem("max_ready")
        nmax_ready = sem("nmax_ready")
        sink_in_ready = sem("sink_in_ready")
        exp_done = sem("exp_done")
        denom_ready = sem("denom_ready")
        rden_ready = sem("rden_ready")
        probs_ready = sem("probs_ready")
        probs_turned = sem("probs_turned")
        probs_t_ready = sem("probs_t_ready")
        pv_done = sem("pv_done")
        attn_ready = sem("attn_ready")
        cat_hi = sem("cat_hi")
        cat_lo = sem("cat_lo")
        wout_done = sem("wout_done")
        y_added = sem("y_added")
        gu_done = sem("gu_done")
        silu_ready = sem("silu_ready")
        hidden_ready = sem("hidden_ready")
        act_hi_ready = sem("act_hi_ready")
        act_lo_ready = sem("act_lo_ready")
        down_done = sem("down_done")
        y_acc = sem("y_acc")

        block = ctx.enter_context(nc.Block())

        def unit_landed(eng, n):
            eng.wait_ge(stage_landed[n % STAGE], 32 * (n // STAGE + 1))

        def unit_parts(n):
            if n < N_PROJ:
                return w_hl[:, 6 + n % 2, 0, :], w_hl[:, 6 + n % 2, 1, :]
            if n < UNIT_FFN:
                return w_hl[:, n - UNIT_WOUT, 0, :], w_hl[:, n - UNIT_WOUT, 1, :]
            k = n - UNIT_FFN
            return gu_a[:, 2 * k, :], gu_a[:, 2 * k + 1, :]

        def chunk_parts(k):
            if k < 2:
                return gu_b[:, 2 * k, :], gu_b[:, 2 * k + 1, :]
            if k < 4:
                return w_dn[:, k - 2, 0, :], w_dn[:, k - 2, 1, :]
            return gu_a[:, 2 * (k - 4), :], gu_a[:, 2 * (k - 4) + 1, :]

        def trans_user_before(t):
            users = [x for x in range(t) if PROJ[x][0] in "vgu" and x % 2 == t % 2]
            return users[-1] if users else None

        def turned_pair(r):
            b = 4 + 2 * (r % 2)
            return ps[:, b:b + 2, :].rearrange("p b (k t) -> p (b k) t", t=P)

        def unit_of(u):
            j, p = divmod(u, 5)
            return j, ([2 * p, 2 * p + 1] if p < 4 else [SAMPLE])

        def unit_shape(u):
            j, rows = unit_of(u)
            return (j, P, 2, P) if len(rows) == 2 else (j, DEC, 1, DEC + DH)

        def stat(tensor, u):
            j, n, tiles, keys = unit_shape(u)
            return tensor[0:n, u % 4, :].rearrange("p (h x) -> p h x", h=2)[:, :, 0:tiles]

        def prob(u):
            j, n, tiles, keys = unit_shape(u)
            return probs[0:n, u % 3, :, :].rearrange("p (h x) c -> p h x c", h=2)[:, :, 0:tiles, 0:keys]

        def score(u):
            j, n, tiles, keys = unit_shape(u)
            b = 2 + 2 * (u % 2)
            return ps[0:n, b:b + 2, 0:2 * P].rearrange("p h (x c) -> p h x c", c=P)[:, :, 0:tiles, 0:keys]

        @block.sync
        def _(sp):
            w_in = a["w_in"][0].rearrange("(k p) c -> p k c", p=P)
            w_out = a["w_out"][0]
            w_gate = a["w_gate"][0].rearrange("(k p) c -> p k c", p=P)
            w_up = a["w_up"][0].rearrange("(k p) c -> p k c", p=P)
            w_down = a["w_down"][0].rearrange("(f p) c -> p f c", p=P)

            def columns(dst, landed, w, c0):
                dst = dst.rearrange("p (k c) -> p k c", k=KT)
                for h in range(2):
                    sp.dma_start(dst[:, 4 * h:4 * h + 4, :],
                                 w[:, 4 * h:4 * h + 4, bass.ds(c0, P)]).then_inc(landed, 16)

            def load_unit(n):
                if n >= STAGE:
                    sp.wait_ge(split_lo, n - STAGE + 1)
                dst, landed = stage[:, n % STAGE, :], stage_landed[n % STAGE]
                if n < N_PROJ:
                    kind, j = PROJ[n]
                    if kind == "q":
                        d3 = dst.rearrange("p (k c) -> p k c", k=KT)
                        for h in range(2):
                            c0 = Q0 + DH * (j + 4 * h)
                            sp.dma_start(d3[:, :, DH * h:DH * h + DH],
                                         w_in[:, :, c0:c0 + DH]).then_inc(landed, 16)
                    else:
                        c0 = {"k": K0, "v": V0, "u": U0, "g": G0}[kind] + P * j
                        columns(dst, landed, w_in, c0)
                elif n < UNIT_FFN:
                    k = n - UNIT_WOUT
                    for h in range(2):
                        r0 = DH * (k + 4 * h) if k < PAIRS else P * k + DH * h
                        sp.dma_start(dst[DH * h:DH * h + DH, :], w_out[r0:r0 + DH, :]).then_inc(landed, 16)
                else:
                    columns(dst, landed, (w_gate, w_up)[n - UNIT_FFN], 0)

            def load_x(i):
                if i >= 4:
                    sp.wait_ge(xn_ready, i - 3)
                sp.dma_start(xin[row_parts(i), i % 4, :], x_rows[i]).then_inc(x_landed[i % 4], 16)

            load_x(0)
            load_x(1)
            load_unit(0)
            load_x(2)
            load_x(3)
            load_unit(1)
            load_unit(2)
            for i in range(4, ROWS):
                load_x(i)
            load_unit(3)
            sp.wait_ge(xn_ready, ROWS)
            sp.dma_start(gain[:, :], a["g_ffn"].partition_broadcast(P) if False else
                         a["g_ffn"][0].partition_broadcast(P)).then_inc(gain_landed, 16)
            for name, cache in (("state_attn_k_sample", "cache_attn_k"), ("state_attn_v_sample", "cache_attn_v")):
                sp.dma_start(o[name][0, 0, 0:P - DEC], a[cache][0, 0, DEC:P]).then_inc(states_out, 16)
            for n in range(4, UNIT_FFN):
                load_unit(n)
                if n == 7:
                    sp.wait_ge(side_freed, SIDE[("turn", "v", 0, 2)] + 1)
                    sp.dma_start(o["state_attn_v_prompt"][0, 0].rearrange("t h d -> t (h d)"),
                                 v_nat[:, 7, :]).then_inc(v_state_out, 16)
                    sp.dma_start(o["state_attn_v_sample"][0, 0, P - DEC:P].rearrange("t h d -> t (h d)"),
                                 v_sample[0:DEC, :]).then_inc(v_state_out, 16)
                if 8 <= n < 8 + GROUPS:
                    g = n - 8
                    sp.wait_ge(vn_ready, ROWS * (g + 1))
                    sp.dma_start(o["state_gmlp_v_sample"][0, 0, :, P * g:P * g + P],
                                 vn[0:DEC, g % 2, SAMPLE, :]).then_inc(g_state_out[g % 2], 16)
                if n == 15:
                    sp.wait_ge(side_freed, SIDE[("turn", "k", 0, 0)] + 1)
                    sp.dma_start(o["state_attn_k_prompt"][0, 0].rearrange("t h d -> t (h d)"),
                                 k_state[:, 0, :]).then_inc(k_state_out, 16)
                    sp.dma_start(o["state_attn_k_sample"][0, 0, P - DEC:P].rearrange("t h d -> t (h d)"),
                                 k_state[0:DEC, 1, :]).then_inc(k_state_out, 16)
            sp.wait_ge(attn_ready, UNITS)
            sp.wait_ge(v_state_out, 32)
            sp.wait_ge(k_state_out, 32)
            for g in range(2):
                sp.wait_ge(g_state_out[g], 32)
            for i in range(7):
                sp.dma_start(y_row(i), x_rows[i]).then_inc(y_landed[i], 16)
            sp.wait_ge(cat_lo, ROWS)
            for i in range(7, ROWS):
                sp.dma_start(y_row(i), x_rows[i]).then_inc(y_landed[i], 16)
            load_unit(UNIT_FFN)
            load_unit(UNIT_FFN + 1)

            def chunk(c, last):
                for k in range(4 if last else 6):
                    sp.wait_ge(split_lo, 6 * c + (UNIT_CHUNK + k - STAGE + 1))
                    n = UNIT_CHUNK + k
                    dst, landed = stage[:, n % STAGE, :], stage_landed[n % STAGE]
                    if k < 2 or k >= 4:
                        tile = 2 * c + (1 if k < 2 else 2)
                        columns(dst, landed, (w_gate, w_up)[k % 2], P * tile)
                    else:
                        for h in range(2):
                            rows = slice(DH * h, DH * h + DH)
                            sp.dma_start(dst[rows, :].unsqueeze(1),
                                         w_down[rows, bass.ds(2 * c + (k - 2), 1), :]).then_inc(landed, 16)

            chunk(0, False)
            sp.wait_ge(xn_ready, 2 * ROWS)
            sp.dma_start(gain[:, :], a["g_final"].partition_broadcast(P)).then_inc(gain_landed, 16)
            with sp.Fori(1, CHUNKS - 1) as c:
                chunk(c, False)
            chunk(CHUNKS - 1, True)
            for i in range(ROWS):
                sp.wait_ge(xn_ready, 2 * ROWS + i + 1)
                sp.dma_start(y_rows[i], xn[row_parts(i), i % 2, :]).then_inc(y_out[i % 2], 16)
            sp.wait_ge(states_out, 32)
            sp.wait_ge(y_out[0], 16 * 5)
            sp.wait_ge(y_out[1], 16 * 4)

        @block.gpsimd
        def _(pool):
            nc.gpsimd.memset(ident[:, :], 0.0).then_inc(pool_consts, 1)
            nc.gpsimd.memset(neg_half[:, :], -0.5).then_inc(pool_consts, 1)
            nc.gpsimd.memset(neg_row[:, :], NEG_BIG).then_inc(pool_consts, 1)
            nc.gpsimd.memset(one_row[:, :], 1.0).then_inc(pool_consts, 1)
            nc.gpsimd.memset(ln_mv[:, :, :], 1.0).then_inc(pool_consts, 1)
            pool.wait_ge(pool_consts, 5)
            nc.gpsimd.affine_select(out=ident[:, :], in_=ident[:, :], compare_op=ALU.not_equal, fill=1.0,
                                    base=0, pattern=[[-1, P]], channel_multiplier=1).then_inc(pool_consts, 1)

            def root(r):
                rows = row_parts(r % ROWS)
                col = slice(r, r + 1)
                if r >= 1:
                    pool.wait_ge(rstd_ready, r)
                if r == ROWS:
                    pool.wait_ge(ln_rstd_ready, GROUPS)
                pool.wait_ge(sumsq_ready, r + 1)
                nc.gpsimd.tensor_scalar(meansq[rows, col], sumsq[rows, col], 1.0 / D, 1e-6,
                                        ALU.mult, ALU.add).then_inc(meansq_ready, 1)
                pool.wait_ge(meansq_ready, r + 1)
                nc.gpsimd.tensor_tensor(rstd[rows, col], meansq[rows, col], neg_half[rows, 0:1],
                                        ALU.pow).then_inc(rstd_ready, 1)

            for item in SCHEDULE:
                if item[0] == "front":
                    if item == ("front", 4):
                        pool.wait_ge(tril_ready, 1)
                    root(item[1])
                if item == ("back", 2):
                    pool.wait_ge(wsp_landed, 16)
                    pool.wait_ge(rstd_ready, 4)
                    nc.gpsimd.affine_select(out=wsp, in_=wsp, compare_op=ALU.is_ge, fill=0.0, base=0,
                                            pattern=[[0, GROUPS], [-1, P]],
                                            channel_multiplier=1).then_inc(tril_ready, 1)
                if item[0] == "turn" and item[1] == "g":
                    g = item[2]
                    pool.wait_ge(ln_aggr, ROWS * (g + 1))
                    if g == 0:
                        pool.wait_ge(rstd_ready, ROWS)
                    else:
                        pool.wait_ge(ln_rstd_ready, g)
                    nc.gpsimd.tensor_scalar(ln_var[:, :], ln_mv[:, :, 1], 1e-5, 1.0,
                                            ALU.add, ALU.mult).then_inc(ln_var_ready, 1)
                    pool.wait_ge(ln_var_ready, g + 1)
                    nc.gpsimd.tensor_tensor(ln_rstd[:, :], ln_var[:, :], neg_half[:, :],
                                            ALU.pow).then_inc(ln_rstd_ready, 1)
            for i in range(ROWS):
                root(2 * ROWS + i)

        @block.tensor
        def _(pe):
            mm, turn = nc.tensor.matmul, nc.tensor.transpose

            def three_passes(out, w_pair, x_pair, first, last):
                (wh, wl), (xh, xl) = w_pair, x_pair
                mm(out, wh, xh, start=first, stop=False)
                mm(out, wh, xl, start=False, stop=False)
                return mm(out, wl, xh, start=False, stop=last)

            def norm_back(r):
                i = r % ROWS
                rows, n = row_parts(i), (P if i != SAMPLE else DEC)
                pe.wait_ge(xn_ready, r + 1)
                if r == 0:
                    pe.wait_ge(pool_consts, 6)
                if r >= 2:
                    pe.wait_ge(lo_ready, r - 1)
                if r == ROWS:
                    pe.wait_ge(attn_ready, UNITS)
                out = turned_pair(r)
                for k in range(KT):
                    t = turn(out[:, k, 0:n], xn[rows, i % 2, P * k:P * k + P], ident[rows, rows])
                t.then_inc(turned, 1)

            def proj_block(n, half):
                t, b = PROJ_BLOCKS[n]
                if half != 1:
                    if b == 0:
                        pe.wait_ge(split_lo, t + 1)
                    if t < 2:
                        pe.wait_ge(lo_ready, 3 * (b + 1))
                    if n >= 4:
                        pe.wait_ge(proj_evac, bank_blocks_before(n))
                hi, lo = unit_parts(t)
                cols = slice(BLK * b, BLK * b + BLK)
                for k in (range(KT) if half is None else range(4 * half, 4 * half + 4)):
                    w = [x[:, P * k:P * k + P] for x in (hi, lo)]
                    last = three_passes(ps[:, proj_bank(n), 0:BLK], w, (t_hi[:, k, cols], t_lo[:, k, cols]),
                                        k == 0, k == KT - 1)
                if half != 0:
                    last.then_inc(proj_done, 1)

            def side_bank(item):
                m = SIDE[item]
                if m == 0:
                    pe.wait_ge(lo_ready, ROWS)
                if m >= 4:
                    pe.wait_ge(side_freed, m - 3)
                return ps[:, 4 + m % 4, :]

            def consts():
                out = side_bank(("consts", "tril"))
                pe.wait_ge(tril_ready, 1)
                for g in range(GROUPS):
                    t = turn(out[:, P * g:P * g + P], wsp[:, g, :], ident[:, :])
                t.then_inc(side_done, 1)
                out = side_bank(("consts", "cache"))
                pe.wait_ge(cache_landed, 32)
                turn(out[:, 0:DH], kc_nat, ident[0:DH, 0:DH]).then_inc(side_done, 1)

            def turn_tile(kind, j):
                if kind == "k":
                    pe.wait_ge(proj_evac, last_block(PROJ.index(("k", 0))))
                    out = side_bank(("turn", "k", 0, 0))
                    turn(out[:, 0:P], k_t[:, row_tokens(7)], ident[:, :])
                    turn(out[0:DEC, P:2 * P], k_t[:, row_tokens(SAMPLE)], ident[:, :]).then_inc(side_done, 1)
                    return
                t_in = PROJ.index((kind, j))
                pe.wait_ge(proj_evac, last_block(t_in))
                src = trans[:, t_in % 2, :]
                for sub in range(3):
                    out = side_bank(("turn", kind, j, sub))
                    for x, i in enumerate(part_rows(sub)):
                        n = P if i != SAMPLE else DEC
                        t = turn(out[0:n, P * x:P * x + P], src[:, row_tokens(i)], ident[:, :])
                    t.then_inc(side_done, 1)

            def mix(g):
                pe.wait_ge(vn_ready, ROWS * (g + 1))
                pe.wait_ge(side_freed, SIDE[("consts", "tril")] + 1)
                for sub in range(3):
                    out = side_bank(("mix", g, sub))
                    for x, i in enumerate(part_rows(sub)):
                        n = P if i != SAMPLE else DEC
                        t = mm(out[:, P * x:P * x + n], vn[0:n, g % 2, i, :], wsp_t[0:n, g, 0:n],
                               start=True, stop=True)
                    t.then_inc(side_done, 1)

            def scores(u):
                j, rows = unit_of(u)
                if u == 0:
                    pe.wait_ge(side_freed, N_SIDE)
                if u % 5 == 0:
                    pe.wait_ge(proj_evac, last_block(PROJ.index(("q", j))))
                if u >= 2:
                    pe.wait_ge(exp_done, u - 1)
                for x, i in enumerate(rows):
                    for h in range(2):
                        out, at = ps[:, 2 + 2 * (u % 2) + h, :], x * P
                        hp = slice(DH * h, DH * h + DH)
                        if i == SAMPLE:
                            q = cat[hp, j, SEQ:TOK]
                            mm(out[0:DEC, at:at + DEC], q, k_t[hp, SEQ:TOK], start=True, stop=True)
                            last = mm(out[0:DEC, at + DEC:at + DEC + DH], q, kc_t[hp, :], start=True, stop=True)
                            continue
                        even, odd = P * i, P * i + DH
                        q = cat[hp, j, even:even + DH]
                        mm(out[0:DH, at:at + DH], q, k_t[hp, even:even + DH], start=True, stop=True)
                        if i == 0:
                            mm(out[0:DH, at + DH:at + P], neg_row[:, :], one_row[:, :], start=True, stop=True)
                        else:
                            mm(out[0:DH, at + DH:at + P], q, k_t[hp, even - DH:even], start=True, stop=True)
                        last = mm(out[DH:P, at:at + P], cat[hp, j, odd:odd + DH], k_t[hp, even:even + P],
                                  start=True, stop=True)
                last.then_inc(scores_done, 1)

            def turn_probs(u):
                j, rows = unit_of(u)
                pe.wait_ge(probs_ready, u + 1)
                if u >= 1:
                    pe.wait_ge(probs_t_ready, u)
                for x, i in enumerate(rows):
                    for h in range(2):
                        at = (2 * h + x) * P
                        if i == SAMPLE:
                            t = turn(ps[0:DEC + DH, 6, at:at + DEC], probs[0:DEC, u % 3, 2 * h, 0:DEC + DH],
                                     ident[0:DEC, 0:DEC])
                        else:
                            t = turn(ps[:, 6, at:at + P], probs[:, u % 3, 2 * h + x, :], ident[:, :])
                t.then_inc(probs_turned, 1)

            def probs_v(u):
                j, rows = unit_of(u)
                pe.wait_ge(probs_t_ready, u + 1)
                if u == 0:
                    pe.wait_ge(v_even_zero, 1)
                if u >= 1:
                    pe.wait_ge(attn_ready, u)
                for x, i in enumerate(rows):
                    for h in range(2):
                        hc = slice(DH * h, DH * h + DH)
                        if i == SAMPLE:
                            n = DEC + DH
                            last = mm(ps[hc, 7, 0:DEC], v_sample[0:n, hc], probs_t[0:n, u % 2, 2 * h, 0:DEC],
                                      start=True, stop=True)
                            continue
                        for half, v in enumerate((v_even, v_nat)):
                            at = P * x + DH * half
                            last = mm(ps[hc, 7, at:at + DH], v[:, i, hc],
                                      probs_t[:, u % 2, 2 * h + x, DH * half:DH * half + DH],
                                      start=True, stop=True)
                last.then_inc(pv_done, 1)

            def tick(t):
                if t < UNITS:
                    scores(t)
                if 0 <= t - 2 < UNITS:
                    turn_probs(t - 2)
                if 0 <= t - 3 < UNITS:
                    probs_v(t - 3)

            def out_proj(i):
                if i == 0:
                    pe.wait_ge(proj_evac, N_BLOCKS)
                if i >= 2:
                    pe.wait_ge(y_added, i - 1)
                pe.wait_ge(cat_lo, i + 1)
                win = row_window(i)
                for k in range(KT):
                    if i == 0:
                        pe.wait_ge(split_lo, UNIT_WOUT + k + 1)
                    x = (t_hi[:, k, win], t_lo[:, k, win])
                    for h in range(2):
                        w = [w_hl[:, k, p, 512 * h:512 * h + 512] for p in range(2)]
                        last = three_passes(ps[:, 2 * (i % 2) + h, :], x, w, k == 0, k == KT - 1)
                last.then_inc(wout_done, 1)

            for item in SCHEDULE:
                kind = item[0]
                if kind == "back":
                    norm_back(item[1])
                elif kind == "block":
                    proj_block(item[1], item[2])
                elif kind == "consts":
                    consts()
                elif kind == "turn":
                    turn_tile(item[1], item[2])
                elif kind == "mix":
                    mix(item[1])
                elif kind == "tick":
                    tick(item[1])
                elif kind == "wout":
                    out_proj(item[1])

            def gate_up(c, s, first):
                f, b = divmod(s, BLOCKS)
                cols = slice(BLK * b, BLK * b + BLK)
                if first:
                    if s < 2:
                        pe.wait_ge(y_added, ROWS)
                        if s == 0:
                            pe.wait_ge(lo_ready, 2 * ROWS - 3)
                    if s == 2:
                        pe.wait_ge(lo_ready, 2 * ROWS)
                if not first or s >= 2:
                    pe.wait_ge(hidden_ready, STEPS * c + (s - 1))
                if b == 0:
                    pe.wait_ge(split_lo, 6 * c + (UNIT_CHUNK + 2 * f))
                for g in range(2):
                    for k in range(KT):
                        w = [gu[f][:, 2 * g + p, P * k:P * k + P] for p in range(2)]
                        last = three_passes(ps[:, 2 * (s % 2) + g, 0:BLK], w,
                                            (t_hi[:, k, cols], t_lo[:, k, cols]), k == 0, k == KT - 1)
                last.then_inc(gu_done, 1)

            def down(c, i, first):
                b = (row_tokens(i).stop - 1) // BLK
                if i < 2:
                    if not first:
                        pe.wait_ge(y_acc, ROWS * c)
                else:
                    pe.wait_ge(y_acc, ROWS * c + (i - 1))
                win = row_window(i)
                for f in range(2):
                    if i in (0, 2, 5) or i == 3:
                        pe.wait_ge(act_lo_ready, STEPS * c + (BLOCKS * f + b + 1))
                    if i == 0:
                        pe.wait_ge(split_lo, 6 * c + (UNIT_CHUNK + 3 + f))
                    x = (act_hi[:, f, win], act_lo[:, f, win])
                    for h in range(2):
                        w = [w_dn[:, f, p, 512 * h:512 * h + 512] for p in range(2)]
                        last = three_passes(ps[:, 4 + 2 * (i % 2) + h, :], x, w, f == 0, f == 1)
                last.then_inc(down_done, 1)

            def chunk(c, first):
                for s in range(STEPS):
                    gate_up(c, s, first)
                    if first and s == 1:
                        norm_back(2 * ROWS - 1)
                for i in range(ROWS):
                    down(c, i, first)

            chunk(0, True)
            with pe.Fori(1, CHUNKS - 1) as c:
                chunk(c, False)
            chunk(CHUNKS - 1, False)

        @block.scalar
        def _(act):
            act.dma_start(gain[:, :], a["g_mix"][0].partition_broadcast(P)).then_inc(gain_landed, 16)
            act.dma_start(wsp, a["gmlp_w_spatial"][0].rearrange("g t s -> t g s")).then_inc(wsp_landed, 16)
            act.dma_start(ln_g, a["gmlp_ln_g"][0].partition_broadcast(P)).then_inc(small_landed, 16)
            act.dma_start(ln_b, a["gmlp_ln_b"][0].partition_broadcast(P)).then_inc(small_landed, 16)
            act.dma_start(bsp[:, :, :], a["gmlp_b_spatial"][0].partition_broadcast(P)).then_inc(small_landed, 16)
            act.dma_start(sink8[:, :], a["attn_sinks"][0].partition_broadcast(P)).then_inc(sink_landed, 16)
            act.dma_start(kc_nat, a["cache_attn_k"][0, 0, DH:P].rearrange("t h d -> t (h d)")).then_inc(cache_landed, 16)
            act.dma_start(v_sample[DEC:DEC + DH, :],
                          a["cache_attn_v"][0, 0, DH:P].rearrange("t h d -> t (h d)")).then_inc(cache_landed, 16)

            def norm_front(r):
                i = r % ROWS
                rows = row_parts(i)
                if r < ROWS:
                    act.wait_ge(x_landed[i % 4], 16 * (i // 4 + 1))
                    src = xin[rows, i % 4, :]
                elif r < 2 * ROWS:
                    act.wait_ge(y_added, i + 1)
                    src = y_row(i)
                else:
                    act.wait_ge(y_acc, ROWS * (CHUNKS - 1) + i + 1)
                    src = y_row(i)
                if r == ROWS:
                    act.wait_ge(cat_lo, ROWS)
                if 2 <= r < 2 * ROWS and r != ROWS:
                    act.wait_ge(turned, r - 1)
                if r >= 2 * ROWS:
                    if i < 2:
                        act.wait_ge(turned, 2 * ROWS)
                    else:
                        act.wait_ge(y_out[i % 2], 16 * (i // 2))
                nc.scalar.activation(xn[rows, i % 2, :], src, ACT.Square,
                                     accum_out=sumsq[rows, r:r + 1]).then_inc(sumsq_ready, 1)

            def norm_back(r):
                i = r % ROWS
                n = P if i != SAMPLE else DEC
                act.wait_ge(turned, r + 1)
                nc.scalar.copy(t_hi[:, :, row_tokens(i)], turned_pair(r)[:, :, 0:n]).then_inc(hi_ready, 1)

            def split(n):
                unit_landed(act, n)
                if 2 <= n < N_PROJ:
                    act.wait_ge(proj_done, last_block(n - 2))
                if n == UNIT_WOUT + 6:
                    act.wait_ge(proj_done, last_block(N_PROJ - 2))
                if n == UNIT_WOUT + 7:
                    act.wait_ge(proj_done, last_block(N_PROJ - 1))
                if n == UNIT_FFN:
                    act.wait_ge(cat_lo, ROWS)
                nc.scalar.copy(unit_parts(n)[0], stage[:, n % STAGE, :]).then_inc(split_hi, 1)

            def evacuate(n):
                t, b = PROJ_BLOCKS[n]
                kind, j = PROJ[t]
                cols = slice(BLK * b, BLK * b + BLK)
                act.wait_ge(proj_done, n + 1)
                src = ps[:, proj_bank(n), 0:BLK]
                if kind in "vgu" and b == 0 and trans_user_before(t) is not None:
                    before = trans_user_before(t)
                    bk, bj = PROJ[before]
                    if bk == "u":
                        act.wait_ge(m_ready, BLOCKS * (bj + 1))
                    else:
                        act.wait_ge(side_done, SIDE[("turn", bk, bj, 2)] + 1)
                if kind == "k":
                    out = nc.scalar.copy(k_t[:, cols], src)
                elif kind == "q":
                    out = nc.scalar.copy(cat[:, j, cols], src)
                elif kind == "v":
                    out = nc.scalar.copy(trans[:, t % 2, cols], src)
                else:
                    out = nc.scalar.activation(trans[:, t % 2, cols], src, ACT.Gelu)
                out.then_inc(proj_evac, 1)

            def tick(u):
                if u >= UNITS:
                    return
                j, n, tiles, keys = unit_shape(u)
                if u == 0:
                    for g in range(2):
                        act.wait_ge(g_state_out[g], 32)
                act.wait_ge(sink_in_ready, u + 1)
                if u >= 3:
                    act.wait_ge(probs_turned, u - 2)
                nc.scalar.activation(stat(sink_exp, u), stat(sink_in, u), ACT.Exp)
                for h in range(2):
                    for x in range(tiles):
                        e = nc.scalar.activation(prob(u)[:, h, x, :], score(u)[:, h, x, :], ACT.Exp,
                                                 bias=stat(nmax, u)[:, h, x:x + 1], scale=SCALE,
                                                 accum_out=stat(psums, u)[:, h, x:x + 1])
                e.then_inc(exp_done, 1)

            def split_cat(i):
                if i == 0:
                    act.wait_ge(proj_done, N_BLOCKS)
                    act.wait_ge(m_ready, GROUPS * BLOCKS)
                act.wait_ge(attn_ready, UNITS - 5 + i // 2 + 1)
                tk = row_tokens(i)
                nc.scalar.copy(t_hi[:, :, tk], cat[:, :, tk]).then_inc(cat_hi, 1)

            for item in SCHEDULE:
                kind = item[0]
                if kind == "front":
                    norm_front(item[1])
                elif kind == "back":
                    norm_back(item[1])
                elif kind == "split":
                    split(item[1])
                elif kind == "evac":
                    evacuate(item[1])
                elif kind == "tick":
                    tick(item[1])
                elif kind == "cat":
                    split_cat(item[1])

            def step(c, s, first):
                act.wait_ge(gu_done, STEPS * c + (s + 1))
                if not first or s >= 2:
                    act.wait_ge(hidden_ready, STEPS * c + (s - 1))
                nc.scalar.activation(silu[:, s % 2, :], ps[:, 2 * (s % 2), 0:BLK], ACT.Silu).then_inc(silu_ready, 1)
                act.wait_ge(hidden_ready, STEPS * c + (s + 1))
                f, b = divmod(s, BLOCKS)
                nc.scalar.copy(act_hi[:, f, BLK * b:BLK * b + BLK], hidden[:, s % 2, :]).then_inc(act_hi_ready, 1)

            def split_chunk(c, k):
                n = UNIT_CHUNK + k
                act.wait_ge(stage_landed[n % STAGE], 64 * c + 32 * (n // STAGE + 1))
                if k >= 4:
                    act.wait_ge(gu_done, STEPS * c + BLOCKS)
                nc.scalar.copy(chunk_parts(k)[0], stage[:, n % STAGE, :]).then_inc(split_hi, 1)

            def chunk(c, first, last):
                for s in range(STEPS):
                    step(c, s, first)
                    if first and s == 1:
                        norm_back(2 * ROWS - 1)
                    if s in (0, 1):
                        split_chunk(c, s)
                    if s in (3, 4):
                        split_chunk(c, s - 1)
                if not last:
                    split_chunk(c, 4)
                    split_chunk(c, 5)

            chunk(0, True, False)
            with act.Fori(1, CHUNKS - 1) as c:
                chunk(c, False, False)
            chunk(CHUNKS - 1, False, True)
            for i in range(ROWS):
                norm_front(2 * ROWS + i)

        @block.vector
        def _(dve):
            def low(out, x, hi):
                return nc.vector.tensor_tensor(out, x, hi.bitcast(F32), ALU.subtract)

            nc.vector.memset(v_even[DH:P, 0, :], 0.0).then_inc(v_even_zero, 1)
            dve.wait_ge(sink_landed, 16)
            by_pair = sink8[:, :].rearrange("p (h j) -> p j h", h=2)
            for x in range(2):
                nc.vector.tensor_copy(sink[:, :, :, x], by_pair).then_inc(sinks_ready, 1)
                nc.vector.tensor_scalar(nsink[:, :, :, x], by_pair, -1.0, None, ALU.mult).then_inc(sinks_ready, 1)

            def norm_front(r):
                i = r % ROWS
                rows = row_parts(i)
                src = xin[rows, i % 4, :] if r < ROWS else y_row(i)
                if i == 0:
                    dve.wait_ge(gain_landed, 16 * (r // ROWS + 1))
                dve.wait_ge(rstd_ready, r + 1)
                nc.vector.scalar_tensor_tensor(out=xn[rows, i % 2, :], in0=src, scalar=rstd[rows, r:r + 1],
                                               in1=gain[rows, :], op0=ALU.mult,
                                               op1=ALU.mult).then_inc(xn_ready, 1)

            def norm_back(r):
                i = r % ROWS
                n = P if i != SAMPLE else DEC
                tk = row_tokens(i)
                dve.wait_ge(hi_ready, r + 1)
                low(t_lo[:, :, tk], turned_pair(r)[:, :, 0:n], t_hi[:, :, tk]).then_inc(lo_ready, 1)

            def split(n):
                dve.wait_ge(split_hi, n + 1)
                hi, lo = unit_parts(n)
                low(lo, stage[:, n % STAGE, :], hi).then_inc(split_lo, 1)

            def side(item):
                m = SIDE[item]
                dve.wait_ge(side_done, m + 1)
                return ps[:, 4 + m % 4, :]

            def consts():
                src = side(("consts", "tril"))
                nc.vector.tensor_copy(wsp_t[:, :, :], src.rearrange("p (g s) -> p g s", g=GROUPS)).then_inc(side_freed, 1)
                src = side(("consts", "cache"))
                nc.vector.tensor_copy(kc_t, src[:, 0:DH]).then_inc(side_freed, 1)

            def turn_tile(kind, g):
                if kind == "k":
                    src = side(("turn", "k", 0, 0))
                    for x in range(2):
                        dve.wait_ge(g_state_out[x], 32)
                    nc.vector.tensor_copy(k_state[:, 0, :], src[:, 0:P]).then_inc(v_copied, 1)
                    nc.vector.tensor_copy(k_state[0:DEC, 1, :], src[0:DEC, P:2 * P]).then_inc(side_freed, 1)
                    return
                if kind == "v":
                    for sub in range(2):
                        src = side(("turn", "v", 0, sub)).rearrange("p (i c) -> p i c", i=4)
                        i0 = 4 * sub
                        nc.vector.tensor_copy(v_nat[:, i0:i0 + 4, :], src).then_inc(v_copied, 1)
                        nc.vector.tensor_copy(v_even[0:DH, i0:i0 + 4, :], src[0:DH, :, :]).then_inc(v_copied, 1)
                        n = 4 - sub
                        nc.vector.tensor_copy(v_even[DH:P, i0 + 1:i0 + 1 + n, :],
                                              src[DH:P, 0:n, :]).then_inc(side_freed, 1)
                    src = side(("turn", "v", 0, 2))
                    nc.vector.tensor_copy(v_sample[0:DEC, :], src[0:DEC, 0:P]).then_inc(side_freed, 1)
                    return
                if g == 0:
                    dve.wait_ge(small_landed, 48)
                    dve.wait_ge(pool_consts, 6)
                if g >= 2:
                    dve.wait_ge(g_state_out[g % 2], 16)
                for sub in range(3):
                    src = side(("turn", "g", g, sub))
                    rows = part_rows(sub)
                    n = P if sub < 2 else DEC
                    for x, i in enumerate(rows):
                        nc.vector.bn_stats(ln_st[0:n, i, :], src[0:n, P * x:P * x + P]).then_inc(ln_stats, 1)
                    for i in rows:
                        dve.wait_ge(ln_stats, ROWS * g + i + 1)
                        nc.vector.bn_aggr(ln_mv[0:n, i, :], ln_st[0:n, i, :]).then_inc(ln_aggr, 1)
                    for x, i in enumerate(rows):
                        dve.wait_ge(ln_aggr, ROWS * g + i + 1)
                        nc.vector.scalar_tensor_tensor(
                            out=vn[0:n, g % 2, i, :], in0=src[0:n, P * x:P * x + P],
                            scalar=ln_mv[0:n, i, 0:1], in1=ln_g[0:n, P * g:P * g + P],
                            op0=ALU.subtract, op1=ALU.mult).then_inc(side_freed if i == rows[-1] else ln_centred, 1)

            def affine(g):
                dve.wait_ge(ln_rstd_ready, g + 1)
                dve.wait_ge(side_freed, SIDE[("turn", "g", g, 2)] + 1)
                for i in range(ROWS):
                    n = P if i != SAMPLE else DEC
                    nc.vector.scalar_tensor_tensor(
                        out=vn[0:n, g % 2, i, :], in0=vn[0:n, g % 2, i, :], scalar=ln_rstd[0:n, i:i + 1],
                        in1=ln_b[0:n, P * g:P * g + P], op0=ALU.mult, op1=ALU.add).then_inc(vn_ready, 1)

            def mix(g):
                for sub in range(3):
                    src = side(("mix", g, sub))
                    if sub < 2:
                        dst = cat[:, PAIRS + g, 512 * sub:512 * sub + 512].rearrange("p (i t) -> p i t", i=4)
                        nc.vector.tensor_tensor(dst, src.rearrange("p (i t) -> p i t", i=4),
                                                bsp[:, g:g + 1, :].to_broadcast([P, 4, P]),
                                                ALU.add).then_inc(side_freed, 1)
                    else:
                        nc.vector.tensor_tensor(cat[:, PAIRS + g, SEQ:TOK], src[:, 0:DEC], bsp[:, g, 0:DEC],
                                                ALU.add).then_inc(side_freed, 1)

            def gate_u(n):
                t, b = PROJ_BLOCKS[n]
                kind, g = PROJ[t]
                if kind != "u":
                    return
                cols = slice(BLK * b, BLK * b + BLK)
                dve.wait_ge(proj_evac, n + 1)
                dve.wait_ge(side_freed, SIDE[("mix", g, 2)] + 1)
                nc.vector.tensor_tensor(cat[:, PAIRS + g, cols], trans[:, t % 2, cols], cat[:, PAIRS + g, cols],
                                        ALU.mult).then_inc(m_ready, 1)

            def maxima(u):
                j, n, tiles, keys = unit_shape(u)
                dve.wait_ge(scores_done, u + 1)
                nc.vector.tensor_reduce(stat(smx, u), score(u), AX_X, ALU.max).then_inc(max_ready, 1)
                dve.wait_ge(max_ready, u + 1)
                if u == 0:
                    dve.wait_ge(sinks_ready, 4)
                nc.vector.scalar_tensor_tensor(out=stat(nmax, u), in0=stat(smx, u), scalar=-SCALE,
                                               in1=nsink[0:n, j, :, 0:tiles], op0=ALU.mult,
                                               op1=ALU.min).then_inc(nmax_ready, 1)
                dve.wait_ge(nmax_ready, u + 1)
                nc.vector.tensor_tensor(stat(sink_in, u), stat(nmax, u), sink[0:n, j, :, 0:tiles],
                                        ALU.add).then_inc(sink_in_ready, 1)

            def normalise(u):
                j, n, tiles, keys = unit_shape(u)
                dve.wait_ge(exp_done, u + 1)
                nc.vector.tensor_tensor(stat(denom, u), stat(psums, u), stat(sink_exp, u),
                                        ALU.add).then_inc(denom_ready, 1)
                dve.wait_ge(denom_ready, u + 1)
                nc.vector.reciprocal(stat(rden, u), stat(denom, u)).then_inc(rden_ready, 1)
                dve.wait_ge(rden_ready, u + 1)
                nc.vector.tensor_tensor(prob(u), prob(u),
                                        stat(rden, u).unsqueeze(3).to_broadcast([n, 2, tiles, keys]),
                                        ALU.mult).then_inc(probs_ready, 1)

            def probs_out(u):
                j, n, tiles, keys = unit_shape(u)
                dve.wait_ge(probs_turned, u + 1)
                src = ps[0:keys, 6, :].rearrange("p (h x c) -> p h x c", h=2, c=P)[:, :, 0:tiles, 0:n]
                dst = probs_t[0:keys, u % 2, :, :].rearrange("p (h x) c -> p h x c", h=2)[:, :, 0:tiles, 0:n]
                nc.vector.tensor_copy(dst, src).then_inc(probs_t_ready, 1)

            def attn_out(u):
                j, rows = unit_of(u)
                dve.wait_ge(pv_done, u + 1)
                t0, t1 = row_tokens(rows[0]).start, row_tokens(rows[-1]).stop
                nc.vector.tensor_copy(cat[:, j, t0:t1], ps[:, 7, 0:t1 - t0]).then_inc(attn_ready, 1)

            def tick(t):
                if t < UNITS:
                    maxima(t)
                if 0 <= t - 1 < UNITS:
                    normalise(t - 1)
                if 0 <= t - 2 < UNITS:
                    probs_out(t - 2)
                if 0 <= t - 3 < UNITS:
                    attn_out(t - 3)

            def split_cat(i):
                tk = row_tokens(i)
                dve.wait_ge(cat_hi, i + 1)
                low(t_lo[:, :, tk], cat[:, :, tk], t_hi[:, :, tk]).then_inc(cat_lo, 1)

            def add_out_proj(i):
                rows = row_parts(i)
                dve.wait_ge(wout_done, i + 1)
                dve.wait_ge(y_landed[i], 16)
                b = 2 * (i % 2)
                nc.vector.tensor_tensor(y_row(i), ps[rows, b:b + 2, :].rearrange("p b c -> p (b c)"), y_row(i),
                                        ALU.add).then_inc(y_added, 1)

            for item in SCHEDULE:
                kind = item[0]
                if kind == "front":
                    norm_front(item[1])
                elif kind == "back":
                    norm_back(item[1])
                elif kind == "split":
                    split(item[1])
                elif kind == "consts":
                    consts()
                elif kind == "turn":
                    turn_tile(item[1], item[2])
                elif kind == "affine":
                    affine(item[1])
                elif kind == "mix":
                    mix(item[1])
                elif kind == "evac":
                    gate_u(item[1])
                elif kind == "tick":
                    tick(item[1])
                elif kind == "cat":
                    split_cat(item[1])
                elif kind == "wout":
                    add_out_proj(item[1])

            def step(c, s, first):
                dve.wait_ge(silu_ready, STEPS * c + (s + 1))
                if not first or s >= 2:
                    dve.wait_ge(act_lo_ready, STEPS * c + (s - 1))
                nc.vector.tensor_tensor(hidden[:, s % 2, :], ps[:, 2 * (s % 2) + 1, 0:BLK], silu[:, s % 2, :],
                                        ALU.mult).then_inc(hidden_ready, 1)
                f, b = divmod(s, BLOCKS)
                cols = slice(BLK * b, BLK * b + BLK)
                dve.wait_ge(act_hi_ready, STEPS * c + (s + 1))
                low(act_lo[:, f, cols], hidden[:, s % 2, :], act_hi[:, f, cols]).then_inc(act_lo_ready, 1)

            def split_chunk(c, k):
                n = UNIT_CHUNK + k
                dve.wait_ge(split_hi, 6 * c + (n + 1))
                hi, lo = chunk_parts(k)
                low(lo, stage[:, n % STAGE, :], hi).then_inc(split_lo, 1)

            def add_down(c, i):
                rows = row_parts(i)
                dve.wait_ge(down_done, ROWS * c + (i + 1))
                b = 4 + 2 * (i % 2)
                nc.vector.tensor_tensor(y_row(i), ps[rows, b:b + 2, :].rearrange("p b c -> p (b c)"), y_row(i),
                                        ALU.add).then_inc(y_acc, 1)

            def chunk(c, first, last):
                for s in range(STEPS):
                    step(c, s, first)
                    if first and s == 1:
                        norm_back(2 * ROWS - 1)
                    if s in (0, 1):
                        split_chunk(c, s)
                    if s in (3, 4):
                        split_chunk(c, s - 1)
                for i in range(ROWS):
                    add_down(c, i)
                    if not last and i in (0, 2):
                        split_chunk(c, 4 + i // 2)
                    if last and i >= 1:
                        norm_front(2 * ROWS + i - 1)

            chunk(0, True, False)
            with dve.Fori(1, CHUNKS - 1) as c:
                chunk(c, False, False)
            chunk(CHUNKS - 1, False, True)
            norm_front(3 * ROWS - 1)


_OUTS = [("y_prompt", (1, SEQ, D)), ("y_sample", (1, DEC, D)),
         ("state_attn_k_prompt", (1, 1, P, 2, DH)), ("state_attn_v_prompt", (1, 1, P, 2, DH)),
         ("state_attn_k_sample", (1, 1, P, 2, DH)), ("state_attn_v_sample", (1, 1, P, 2, DH)),
         ("state_gmlp_v_sample", (1, 1, DEC, GROUPS * P))]


def kernel(**inputs):
    import numpy as _np
    import concourse.bacc as _bacc
    from concourse.bass_utils import run_bass_kernel_spmd as _run

    nc = _bacc.Bacc("TRN2", target_bir_lowering=False, num_devices=1, dynamic_dma_scratch_size=1024)
    arrays, ins, outs = {}, {}, {}
    for name, value in inputs.items():
        arr = _np.ascontiguousarray(value)
        arrays[f"in_{name}"] = arr
        ins[name] = nc.dram_tensor(f"in_{name}", arr.shape, mybir.dt.from_np(arr.dtype), kind="ExternalInput").ap()
    for name, shape in _OUTS:
        outs[name] = nc.dram_tensor(f"out_{name}", shape, F32, kind="ExternalOutput").ap()
    build(nc, ins, outs)
    r = _run(nc, [arrays], core_ids=[0])
    return tuple(r.results[0][f"out_{name}"] for name, _ in _OUTS)
```

```python
from contextlib import ExitStack

import concourse.bass as bass
from concourse import mybir

F32 = mybir.dt.float32
F32R = mybir.dt.float32r
ALU = mybir.AluOpType
ACT = mybir.ActivationFunctionType
AX_X = mybir.AxisListType.X

P = 128
D = 1024
SEQ, DEC = 1024, 32
TOK = SEQ + DEC
ROWS = SEQ // P + 1
SAMPLE = ROWS - 1
BLOCKS = 3
BLK = TOK // BLOCKS
KT = D // P
DH = 64
N_HEADS = 8
PAIRS = 4
OUT_RING = 6
GROUPS = 4
Q0, K0, V0, U0, G0 = 0, 512, 640, 768, 1280
SCALE = DH ** -0.5
NEG_BIG = -1e30
D_FF = 2816
CHUNKS = D_FF // (2 * P)
STEPS = 2 * BLOCKS

PROJ = [("v", 0), ("g", 0), ("g", 1), ("g", 2), ("g", 3), ("u", 0), ("u", 1),
        ("k", 0), ("q", 0), ("q", 1), ("q", 2), ("q", 3), ("u", 2), ("u", 3)]
LATE_U = 12
PROJ_BLOCKS = [(0, 0), (1, 0), (0, 1), (1, 1), (0, 2), (1, 2)] + [
    (t, b) for t in range(2, len(PROJ)) for b in range(BLOCKS)]
N_PROJ = len(PROJ)
N_BLOCKS = len(PROJ_BLOCKS)
ATTN_BLOCK = PROJ_BLOCKS.index((PROJ.index(("q", 1)), 0))


def proj_bank(n):
    return n % 4 if n < ATTN_BLOCK else n % 2


def bank_blocks_before(n):
    return n - 3 if n < ATTN_BLOCK else n - 1


STAGE = 3
UNIT_WOUT = N_PROJ
UNIT_FFN = UNIT_WOUT + KT
UNIT_CHUNK = UNIT_FFN + 2

UNITS = 5 * PAIRS


def last_block(t):
    return max(n for n, (tt, _) in enumerate(PROJ_BLOCKS) if tt == t) + 1


def make_schedule():
    s = [("front", 0), ("front", 1), ("back", 0), ("front", 2), ("split", 0), ("back", 1),
         ("front", 3), ("back", 2), ("block", 0, None), ("split", 1), ("front", 4), ("back", 3),
         ("block", 1, None), ("front", 5), ("back", 4), ("front", 6), ("back", 5), ("evac", 0),
         ("block", 2, None), ("front", 7), ("back", 6), ("evac", 1), ("block", 3, None),
         ("front", 8), ("back", 7), ("back", 8), ("evac", 2), ("block", 4, None), ("evac", 3),
         ("block", 5, None), ("evac", 4), ("split", 2), ("evac", 5), ("split", 3)]
    turn = {("v", 0): 6, ("k", 0): 25}
    turn.update({("g", g): 3 * g + 7 for g in range(GROUPS)})
    w_out_after = {16: 0, 19: 1, 22: 2, 25: 3, 28: 4, 31: 5, 38: 6}
    q1 = PROJ.index(("q", 1))
    for n in range(6, N_BLOCKS):
        t, b = PROJ_BLOCKS[n]
        if q1 <= t < q1 + PAIRS:
            first = 5 * (t - q1) + 2 * b
            s += [("block", n, 0), ("tick", first), ("block", n, 1), ("evac", n)]
            if b < 2:
                s.append(("tick", first + 1))
        elif n == N_BLOCKS - 3:
            s += [("block", n, 0), ("tick", UNITS), ("block", n, 1), ("evac", n), ("tick", UNITS + 1)]
        elif n == N_BLOCKS - 2:
            s += [("block", n, 0), ("tick", UNITS + 2), ("block", n, 1), ("evac", n), ("cat", 0), ("cat", 1)]
        else:
            s.append(("block", n, None))
            if n == 6:
                s.append(("consts",))
            for what, at in turn.items():
                if at == n:
                    s.append(("turn",) + what)
            s.append(("evac", n))
        for g in range(GROUPS):
            if n == 3 * g + 8:
                s.append(("affine", g))
            if n == 3 * g + 11:
                s.append(("mix", g))
        if b == BLOCKS - 1 and t + 2 < N_PROJ:
            s.append(("split", t + 2))
        if b == BLOCKS - 1 and t == LATE_U:
            s.append(("late",))
        if n in w_out_after:
            s.append(("split", UNIT_WOUT + w_out_after[n]))
    s += [("cat", 2), ("split", UNIT_WOUT + 7)]
    for i in range(3, ROWS):
        s.append(("cat", i))
    for i in range(ROWS):
        s.append(("wout", i))
        if i >= 1:
            s.append(("back", ROWS + i - 1))
        s.append(("front", ROWS + i))
        if i == 5:
            s += [("split", UNIT_FFN), ("split", UNIT_FFN + 1)]
    return s


SCHEDULE = make_schedule()
STAGED = [item[1] for item in SCHEDULE if item[0] == "split"]
PLACE = {unit: n for n, unit in enumerate(STAGED)}


def side_parts(item):
    kind = item[0]
    if kind == "consts":
        return ["tril", "cache"]
    if kind == "turn":
        return [0] if item[1] == "k" else [0, 1, 2]
    if kind == "mix":
        return [0, 1, 2]
    return []


SIDE = {}
for _item in SCHEDULE:
    for _part in side_parts(_item):
        SIDE[_item + (_part,)] = len(SIDE)
N_SIDE = len(SIDE)


def part_rows(sub):
    return [range(0, 4), range(4, 8), range(8, 9)][sub]


def row_parts(i):
    return slice(0, P if i != SAMPLE else DEC)


def row_tokens(i):
    return slice(P * i, P * i + (P if i != SAMPLE else DEC))


def build(nc, a, o):
    x_rows = [a["x_prompt"][0, P * i:P * i + P, :] for i in range(SAMPLE)] + [a["x_sample"][0]]
    y_rows = [o["y_prompt"][0, P * i:P * i + P, :] for i in range(SAMPLE)] + [o["y_sample"][0]]

    with ExitStack() as ctx:
        def sb(name, shape, dt=F32):
            return ctx.enter_context(nc.sbuf_tensor(name, shape, dt))

        def sem(name):
            return ctx.enter_context(nc.semaphore(name))

        WORK = 15616
        work_at = -(-nc.sbuf_base // 32) * 32
        work = sb("work", [P, WORK])
        trans_at = -(-nc.sbuf_base // 32) * 32
        trans = sb("trans", [P, 2, TOK])
        sample_cat = nc.alloc_sbuf_tensor_at("sample_cat", [P, KT, 2, DEC], F32R, offset=trans_at)
        gu_a = nc.alloc_sbuf_tensor_at("gate_up_a", [P, 4, D], F32R, offset=work_at + 4 * 2048)
        t_hl = sb("t_hl", [P, 2, KT, TOK], F32R)
        wbuf = sb("wbuf", [P, KT * 2 * D], F32R)
        stage = sb("stage", [P, STAGE, D])
        gain = sb("gain", [P, D])
        wsp_t = sb("wsp_t", [P, GROUPS, P])
        bsp = sb("bsp", [P, GROUPS, P])
        ident = sb("ident", [P, P])
        neg_half = sb("neg_half", [P, 9])
        neg_row = sb("neg_row", [1, DH])
        one_row = sb("one_row", [1, DH])
        sumsq = sb("sumsq", [P, 3 * ROWS])
        meansq = sb("meansq", [P, 3 * ROWS])
        rstd = sb("rstd", [P, 3 * ROWS])
        ln_st = sb("ln_st", [P, ROWS, 6])
        ln_mv = sb("ln_mv", [P, ROWS, 2])
        ln_var = sb("ln_var", [P, ROWS])
        ln_rstd = sb("ln_rstd", [P, ROWS])
        sink8 = sb("sink8", [P, N_HEADS])
        sink = sb("sink", [P, PAIRS, 2, 2])
        nsink = sb("nsink", [P, PAIRS, 2, 2])
        smx = sb("smx", [P, 4, 4])
        nmax = sb("nmax", [P, 4, 4])
        sink_in = sb("sink_in", [P, 4, 4])
        sink_exp = sb("sink_exp", [P, 4, 4])
        psums = sb("psums", [P, 4, 4])
        denom = sb("denom", [P, 4, 4])
        rden = sb("rden", [P, 4, 4])

        cat = work[:, 0:8448].rearrange("p (k t) -> p k t", k=8)
        xn = work[:, 0:2048].rearrange("p (s c) -> p s c", s=2)
        xo = work[:, 0:6144].rearrange("p (s c) -> p s c", s=OUT_RING)
        xin = work[:, 4224:4224 + 4096].rearrange("p (s c) -> p s c", s=4)
        k_t = work[:, 8448:9504]
        v_nat = work[:, 9504:10528].rearrange("p (i c) -> p i c", i=8)
        v_even = work[:, 10528:11552].rearrange("p (i c) -> p i c", i=8)
        v_sample = work[:, 11552:11680]
        kc_t = work[:, 11680:11744]
        ln_g = work[:, 11872:12384]
        ln_b = work[:, 12384:12896]
        vn = work[:, 13312:15616].rearrange("p (s i c) -> p s i c", s=2, i=ROWS)
        wsp = work[:, 13312:13824].rearrange("p (g s) -> p g s", g=GROUPS)
        kc_nat = work[0:DH, 15488:15616]
        probs = work[:, 11872:13408].rearrange("p (s h c) -> p s h c", s=3, h=4)
        probs_t = work[:, 13408:14432].rearrange("p (s h c) -> p s h c", s=2, h=4)
        k_state = work[:, 14432:14688].rearrange("p (s c) -> p s c", s=2)
        y_slots = work[:, 6400:15616].rearrange("p (s c) -> p s c", s=ROWS)

        def y_row(i):
            return y_slots[row_parts(i), (i + 2) % ROWS, :]

        w_hl = wbuf[:, :].rearrange("p (s h c) -> p s h c", s=KT, h=2)
        t_hi, t_lo = t_hl[:, 0, :, :], t_hl[:, 1, :, :]
        act_hl = wbuf[:, 0:4 * TOK].rearrange("p (h f t) -> p h f t", h=2, f=2)
        sample_act = wbuf[:, 12416:12416 + 4 * DEC].rearrange("p (f h t) -> p f h t", f=2, h=2)
        act_hi, act_lo = act_hl[:, 0, :, :], act_hl[:, 1, :, :]
        w_dn = wbuf[:, 4224:8320].rearrange("p (f h c) -> p f h c", f=2, h=2)
        gu_b = wbuf[:, 8320:12416].rearrange("p (s c) -> p s c", s=4)
        gu = [gu_a[:, :, :], gu_b]
        silu = trans[:, 0, 0:2 * BLK].rearrange("p (s c) -> p s c", s=2)
        hidden = trans[:, 1, 0:2 * BLK].rearrange("p (s c) -> p s c", s=2)

        ps = ctx.enter_context(nc.psum_tensor("ps", [P, 8, 512], F32))

        x_landed = [sem(f"x_landed{i}") for i in range(4)]
        y_landed = [sem(f"y_landed{i}") for i in range(ROWS)]
        stage_landed = [sem(f"stage_landed{i}") for i in range(STAGE)]
        gain_landed = sem("gain_landed")
        wsp_landed = sem("wsp_landed")
        small_landed = sem("small_landed")
        sink_landed = sem("sink_landed")
        cache_landed = sem("cache_landed")
        states_out = sem("states_out")
        v_state_out = sem("v_state_out")
        k_state_out = sem("k_state_out")
        g_state_out = [sem(f"g_state_out{i}") for i in range(2)]
        y_out = [sem(f"y_out{i}") for i in range(OUT_RING)]
        pool_consts = sem("pool_consts")
        tril_ready = sem("tril_ready")
        sumsq_ready = sem("sumsq_ready")
        meansq_ready = sem("meansq_ready")
        rstd_ready = sem("rstd_ready")
        xn_ready = sem("xn_ready")
        turned = sem("turned")
        hi_ready = sem("hi_ready")
        lo_ready = sem("lo_ready")
        split_hi = sem("split_hi")
        split_lo = sem("split_lo")
        proj_done = sem("proj_done")
        proj_evac = sem("proj_evac")
        side_done = sem("side_done")
        side_freed = sem("side_freed")
        v_even_zero = sem("v_even_zero")
        v_copied = sem("v_copied")
        ln_stats = sem("ln_stats")
        ln_aggr = sem("ln_aggr")
        ln_centred = sem("ln_centred")
        ln_var_ready = sem("ln_var_ready")
        ln_rstd_ready = sem("ln_rstd_ready")
        vn_ready = sem("vn_ready")
        m_ready = sem("m_ready")
        late_gelu_done = sem("late_gelu_done")
        sinks_ready = sem("sinks_ready")
        scores_done = sem("scores_done")
        max_ready = sem("max_ready")
        nmax_ready = sem("nmax_ready")
        sink_in_ready = sem("sink_in_ready")
        exp_done = sem("exp_done")
        denom_ready = sem("denom_ready")
        rden_ready = sem("rden_ready")
        probs_ready = sem("probs_ready")
        probs_turned = sem("probs_turned")
        probs_t_ready = sem("probs_t_ready")
        pv_done = sem("pv_done")
        attn_ready = sem("attn_ready")
        cat_hi = sem("cat_hi")
        cat_lo = sem("cat_lo")
        wout_done = sem("wout_done")
        y_added = sem("y_added")
        low_added = sem("low_added")
        sample_ready = sem("sample_ready")
        gu_done = sem("gu_done")
        silu_ready = sem("silu_ready")
        hidden_ready = sem("hidden_ready")
        act_hi_ready = sem("act_hi_ready")
        act_lo_ready = sem("act_lo_ready")
        down_done = sem("down_done")
        y_acc = sem("y_acc")

        block = ctx.enter_context(nc.Block())

        def unit_landed(eng, n):
            eng.wait_ge(stage_landed[PLACE[n] % STAGE], 32 * (PLACE[n] // STAGE + 1))

        def unit_stage(n):
            return stage[:, PLACE[n] % STAGE, :]

        def unit_parts(n):
            if n < N_PROJ:
                return w_hl[:, 6 + n % 2, 0, :], w_hl[:, 6 + n % 2, 1, :]
            if n < UNIT_FFN:
                return w_hl[:, n - UNIT_WOUT, 0, :], w_hl[:, n - UNIT_WOUT, 1, :]
            k = n - UNIT_FFN
            return gu_a[:, 2 * k, :], gu_a[:, 2 * k + 1, :]

        def chunk_parts(k):
            if k < 2:
                return gu_b[:, 2 * k, :], gu_b[:, 2 * k + 1, :]
            if k < 4:
                return w_dn[:, k - 2, 0, :], w_dn[:, k - 2, 1, :]
            return gu_a[:, 2 * (k - 4), :], gu_a[:, 2 * (k - 4) + 1, :]

        def gate_bank(s):
            return 2 * ((s + 1) % 2)

        def trans_user_before(t):
            users = [x for x in range(t) if PROJ[x][0] in "vgu" and x % 2 == t % 2]
            return users[-1] if users else None

        def turned_pair(r):
            b = 4 + 2 * (r % 2)
            return ps[:, b:b + 2, :].rearrange("p b (k t) -> p (b k) t", t=P)

        def unit_of(u):
            j, p = divmod(u, 5)
            return j, ([2 * p, 2 * p + 1] if p < 4 else [SAMPLE])

        def unit_shape(u):
            j, rows = unit_of(u)
            return (j, P, 2, P) if len(rows) == 2 else (j, DEC, 1, DEC + DH)

        def stat(tensor, u):
            j, n, tiles, keys = unit_shape(u)
            return tensor[0:n, u % 4, :].rearrange("p (h x) -> p h x", h=2)[:, :, 0:tiles]

        def prob(u):
            j, n, tiles, keys = unit_shape(u)
            return probs[0:n, u % 3, :, :].rearrange("p (h x) c -> p h x c", h=2)[:, :, 0:tiles, 0:keys]

        def score(u):
            j, n, tiles, keys = unit_shape(u)
            b = 2 + 2 * (u % 2)
            return ps[0:n, b:b + 2, 0:2 * P].rearrange("p h (x c) -> p h x c", c=P)[:, :, 0:tiles, 0:keys]

        @block.sync
        def _(sp):
            w_in = a["w_in"][0].rearrange("(k p) c -> p k c", p=P)
            w_out = a["w_out"][0]
            w_gate = a["w_gate"][0].rearrange("(k p) c -> p k c", p=P)
            w_up = a["w_up"][0].rearrange("(k p) c -> p k c", p=P)
            w_down = a["w_down"][0].rearrange("(f p) c -> p f c", p=P)

            def columns(dst, landed, w, c0):
                dst = dst.rearrange("p (k c) -> p k c", k=KT)
                for h in range(2):
                    sp.dma_start(dst[:, 4 * h:4 * h + 4, :],
                                 w[:, 4 * h:4 * h + 4, bass.ds(c0, P)]).then_inc(landed, 16)

            def load_unit(n):
                if PLACE[n] >= STAGE:
                    sp.wait_ge(split_lo, PLACE[n] - STAGE + 1)
                dst, landed = unit_stage(n), stage_landed[PLACE[n] % STAGE]
                if n < N_PROJ:
                    kind, j = PROJ[n]
                    if kind == "q":
                        d3 = dst.rearrange("p (k c) -> p k c", k=KT)
                        for h in range(2):
                            c0 = Q0 + DH * (j + 4 * h)
                            sp.dma_start(d3[:, :, DH * h:DH * h + DH],
                                         w_in[:, :, c0:c0 + DH]).then_inc(landed, 16)
                    else:
                        c0 = {"k": K0, "v": V0, "u": U0, "g": G0}[kind] + P * j
                        columns(dst, landed, w_in, c0)
                elif n < UNIT_FFN:
                    k = n - UNIT_WOUT
                    for h in range(2):
                        r0 = DH * (k + 4 * h) if k < PAIRS else P * k + DH * h
                        sp.dma_start(dst[DH * h:DH * h + DH, :], w_out[r0:r0 + DH, :]).then_inc(landed, 16)
                else:
                    columns(dst, landed, (w_gate, w_up)[n - UNIT_FFN], 0)

            def load_x(i):
                if i >= 4:
                    sp.wait_ge(xn_ready, i - 3)
                sp.dma_start(xin[row_parts(i), i % 4, :], x_rows[i]).then_inc(x_landed[i % 4], 16)

            load_x(0)
            sp.dma_start(gain[:, :], a["g_mix"][0].partition_broadcast(P)).then_inc(gain_landed, 16)
            load_x(1)
            load_x(2)
            load_unit(0)
            load_x(3)
            load_unit(1)
            sp.dma_start(wsp, a["gmlp_w_spatial"][0].rearrange("g t s -> t g s")).then_inc(wsp_landed, 16)
            load_x(4)
            load_x(5)
            load_unit(2)
            load_x(6)
            load_x(7)
            load_x(8)
            sp.dma_start(ln_g, a["gmlp_ln_g"][0].partition_broadcast(P)).then_inc(small_landed, 16)
            sp.dma_start(ln_b, a["gmlp_ln_b"][0].partition_broadcast(P)).then_inc(small_landed, 16)
            sp.dma_start(bsp[:, :, :], a["gmlp_b_spatial"][0].partition_broadcast(P)).then_inc(small_landed, 16)
            sp.dma_start(kc_nat, a["cache_attn_k"][0, 0, DH:P].rearrange("t h d -> t (h d)")).then_inc(cache_landed, 16)
            sp.dma_start(v_sample[DEC:DEC + DH, :],
                         a["cache_attn_v"][0, 0, DH:P].rearrange("t h d -> t (h d)")).then_inc(cache_landed, 16)
            load_unit(3)
            sp.dma_start(sink8[:, :], a["attn_sinks"][0].partition_broadcast(P)).then_inc(sink_landed, 16)
            sp.wait_ge(xn_ready, ROWS)
            sp.dma_start(gain[:, :], a["g_ffn"][0].partition_broadcast(P)).then_inc(gain_landed, 16)
            for name, cache in (("state_attn_k_sample", "cache_attn_k"), ("state_attn_v_sample", "cache_attn_v")):
                sp.dma_start(o[name][0, 0, 0:P - DEC], a[cache][0, 0, DEC:P]).then_inc(states_out, 16)
            g_state_after = {8: 0, 9: 1, 10: 2, 12: 3}
            for n in range(4, UNIT_FFN):
                load_unit(STAGED[n])
                if n == 7:
                    sp.wait_ge(side_freed, SIDE[("turn", "v", 0, 2)] + 1)
                    sp.dma_start(o["state_attn_v_prompt"][0, 0].rearrange("t h d -> t (h d)"),
                                 v_nat[:, 7, :]).then_inc(v_state_out, 16)
                    sp.dma_start(o["state_attn_v_sample"][0, 0, P - DEC:P].rearrange("t h d -> t (h d)"),
                                 v_sample[0:DEC, :]).then_inc(v_state_out, 16)
                if n in g_state_after:
                    g = g_state_after[n]
                    sp.wait_ge(vn_ready, ROWS * (g + 1))
                    sp.dma_start(o["state_gmlp_v_sample"][0, 0, :, P * g:P * g + P],
                                 vn[0:DEC, g % 2, SAMPLE, :]).then_inc(g_state_out[g % 2], 16)
                if n == 16:
                    sp.wait_ge(side_freed, SIDE[("turn", "k", 0, 0)] + 1)
                    sp.dma_start(o["state_attn_k_prompt"][0, 0].rearrange("t h d -> t (h d)"),
                                 k_state[:, 0, :]).then_inc(k_state_out, 16)
                    sp.dma_start(o["state_attn_k_sample"][0, 0, P - DEC:P].rearrange("t h d -> t (h d)"),
                                 k_state[0:DEC, 1, :]).then_inc(k_state_out, 16)
            sp.wait_ge(attn_ready, UNITS)
            sp.wait_ge(v_state_out, 32)
            sp.wait_ge(k_state_out, 32)
            for g in range(2):
                sp.wait_ge(g_state_out[g], 32)
            for i in range(7):
                sp.dma_start(y_row(i), x_rows[i]).then_inc(y_landed[i], 16)
            sp.wait_ge(cat_lo, ROWS)
            for i in range(7, ROWS):
                sp.dma_start(y_row(i), x_rows[i]).then_inc(y_landed[i], 16)
            load_unit(UNIT_FFN)
            load_unit(UNIT_FFN + 1)

            def chunk(c, last):
                for k in range(4 if last else 6):
                    sp.wait_ge(split_lo, 6 * c + (UNIT_CHUNK + k - STAGE + 1))
                    n = UNIT_CHUNK + k
                    dst, landed = stage[:, n % STAGE, :], stage_landed[n % STAGE]
                    if k < 2 or k >= 4:
                        tile = 2 * c + (1 if k < 2 else 2)
                        columns(dst, landed, (w_gate, w_up)[k % 2], P * tile)
                    else:
                        for h in range(2):
                            rows = slice(DH * h, DH * h + DH)
                            sp.dma_start(dst[rows, :].unsqueeze(1),
                                         w_down[rows, bass.ds(2 * c + (k - 2), 1), :]).then_inc(landed, 16)

            chunk(0, False)
            sp.wait_ge(xn_ready, 2 * ROWS)
            sp.dma_start(gain[:, :], a["g_final"].partition_broadcast(P)).then_inc(gain_landed, 16)
            with sp.Fori(1, CHUNKS - 1) as c:
                chunk(c, False)
            chunk(CHUNKS - 1, True)
            for i in range(ROWS):
                sp.wait_ge(xn_ready, 2 * ROWS + i + 1)
                sp.dma_start(y_rows[i], xo[row_parts(i), i % OUT_RING, :]).then_inc(y_out[i % OUT_RING], 16)
            sp.wait_ge(states_out, 32)
            for r in range(OUT_RING):
                sp.wait_ge(y_out[r], 16 * len(range(r, ROWS, OUT_RING)))

        @block.gpsimd
        def _(pool):
            nc.gpsimd.memset(ident[:, :], 0.0).then_inc(pool_consts, 1)
            nc.gpsimd.memset(neg_half[:, :], -0.5).then_inc(pool_consts, 1)
            nc.gpsimd.memset(neg_row[:, :], NEG_BIG).then_inc(pool_consts, 1)
            nc.gpsimd.memset(one_row[:, :], 1.0).then_inc(pool_consts, 1)
            nc.gpsimd.memset(ln_mv[:, :, :], 1.0).then_inc(pool_consts, 1)
            pool.wait_ge(pool_consts, 5)
            nc.gpsimd.affine_select(out=ident[:, :], in_=ident[:, :], compare_op=ALU.not_equal, fill=1.0,
                                    base=0, pattern=[[-1, P]], channel_multiplier=1).then_inc(pool_consts, 1)

            def root(r):
                rows = row_parts(r % ROWS)
                col = slice(r, r + 1)
                if r >= 1:
                    pool.wait_ge(rstd_ready, r)
                if r == ROWS:
                    pool.wait_ge(ln_rstd_ready, GROUPS)
                pool.wait_ge(sumsq_ready, r + 1)
                nc.gpsimd.tensor_scalar(meansq[rows, col], sumsq[rows, col], 1.0 / D, 1e-6,
                                        ALU.mult, ALU.add).then_inc(meansq_ready, 1)
                pool.wait_ge(meansq_ready, r + 1)
                nc.gpsimd.tensor_tensor(rstd[rows, col], meansq[rows, col], neg_half[rows, 0:1],
                                        ALU.pow).then_inc(rstd_ready, 1)

            for item in SCHEDULE:
                if item[0] == "front":
                    if item == ("front", 4):
                        pool.wait_ge(tril_ready, 1)
                    root(item[1])
                if item == ("back", 2):
                    pool.wait_ge(wsp_landed, 16)
                    pool.wait_ge(rstd_ready, 4)
                    nc.gpsimd.affine_select(out=wsp, in_=wsp, compare_op=ALU.is_ge, fill=0.0, base=0,
                                            pattern=[[0, GROUPS], [-1, P]],
                                            channel_multiplier=1).then_inc(tril_ready, 1)
                if item[0] == "turn" and item[1] == "g":
                    g = item[2]
                    pool.wait_ge(ln_aggr, ROWS * (g + 1))
                    if g == 0:
                        pool.wait_ge(rstd_ready, ROWS)
                    else:
                        pool.wait_ge(ln_rstd_ready, g)
                    nc.gpsimd.tensor_scalar(ln_var[:, :], ln_mv[:, :, 1], 1e-5, 1.0,
                                            ALU.add, ALU.mult).then_inc(ln_var_ready, 1)
                    pool.wait_ge(ln_var_ready, g + 1)
                    nc.gpsimd.tensor_tensor(ln_rstd[:, :], ln_var[:, :], neg_half[:, :],
                                            ALU.pow).then_inc(ln_rstd_ready, 1)
            for i in range(ROWS):
                root(2 * ROWS + i)

        @block.tensor
        def _(pe):
            mm, turn = nc.tensor.matmul, nc.tensor.transpose

            def three_passes(out, w_pair, x_pair, first, last):
                (wh, wl), (xh, xl) = w_pair, x_pair
                mm(out, wh, xh, start=first, stop=False)
                mm(out, wh, xl, start=False, stop=False)
                return mm(out, wl, xh, start=False, stop=last)

            def row_products(i, k, x_hl, sample_hl, w, b, first, last):
                for h in range(2):
                    w_hi, w_lo = [w[:, p, 512 * h:512 * h + 512] for p in range(2)]
                    tk = row_tokens(i)
                    if i != SAMPLE:
                        x_hi, x_lo = x_hl[:, 0, k, tk], x_hl[:, 1, k, tk]
                        t = three_passes(ps[:, b + h, :], (x_hi, x_lo), (w_hi, w_lo), first, last)
                    else:
                        x_both = sample_hl[:, k, :, :].rearrange("p h t -> p (h t)")
                        out = ps[0:2 * DEC, b + h, :]
                        mm(out, x_both, w_hi, start=first, stop=False)
                        t = mm(out, x_both, w_lo, start=False, stop=last)
                return t

            def norm_back(r):
                i = r % ROWS
                rows, n = row_parts(i), (P if i != SAMPLE else DEC)
                pe.wait_ge(xn_ready, r + 1)
                if r == 0:
                    pe.wait_ge(pool_consts, 6)
                if r >= 2:
                    pe.wait_ge(lo_ready, r - 1)
                if r == ROWS:
                    pe.wait_ge(attn_ready, UNITS)
                out = turned_pair(r)
                for k in range(KT):
                    t = turn(out[:, k, 0:n], xn[rows, i % 2, P * k:P * k + P], ident[rows, rows])
                t.then_inc(turned, 1)

            def proj_block(n, half):
                t, b = PROJ_BLOCKS[n]
                if half != 1:
                    if b == 0:
                        pe.wait_ge(split_lo, PLACE[t] + 1)
                    if t < 2:
                        pe.wait_ge(lo_ready, 3 * (b + 1))
                    if n >= 4:
                        pe.wait_ge(proj_evac, bank_blocks_before(n))
                hi, lo = unit_parts(t)
                cols = slice(BLK * b, BLK * b + BLK)
                for k in (range(KT) if half is None else range(4 * half, 4 * half + 4)):
                    w = [x[:, P * k:P * k + P] for x in (hi, lo)]
                    last = three_passes(ps[:, proj_bank(n), 0:BLK], w, (t_hi[:, k, cols], t_lo[:, k, cols]),
                                        k == 0, k == KT - 1)
                if half != 0:
                    last.then_inc(proj_done, 1)

            def side_bank(item):
                m = SIDE[item]
                if m == 0:
                    pe.wait_ge(lo_ready, ROWS)
                if m >= 4:
                    pe.wait_ge(side_freed, m - 3)
                return ps[:, 4 + m % 4, :]

            def consts():
                out = side_bank(("consts", "tril"))
                pe.wait_ge(tril_ready, 1)
                for g in range(GROUPS):
                    t = turn(out[:, P * g:P * g + P], wsp[:, g, :], ident[:, :])
                t.then_inc(side_done, 1)
                out = side_bank(("consts", "cache"))
                pe.wait_ge(cache_landed, 32)
                turn(out[:, 0:DH], kc_nat, ident[0:DH, 0:DH]).then_inc(side_done, 1)

            def turn_tile(kind, j):
                if kind == "k":
                    pe.wait_ge(proj_evac, last_block(PROJ.index(("k", 0))))
                    out = side_bank(("turn", "k", 0, 0))
                    turn(out[:, 0:P], k_t[:, row_tokens(7)], ident[:, :])
                    turn(out[0:DEC, P:2 * P], k_t[:, row_tokens(SAMPLE)], ident[:, :]).then_inc(side_done, 1)
                    return
                t_in = PROJ.index((kind, j))
                pe.wait_ge(proj_evac, last_block(t_in))
                src = trans[:, t_in % 2, :]
                for sub in range(3):
                    out = side_bank(("turn", kind, j, sub))
                    for x, i in enumerate(part_rows(sub)):
                        n = P if i != SAMPLE else DEC
                        t = turn(out[0:n, P * x:P * x + P], src[:, row_tokens(i)], ident[:, :])
                    t.then_inc(side_done, 1)

            def mix(g):
                pe.wait_ge(vn_ready, ROWS * (g + 1))
                pe.wait_ge(side_freed, SIDE[("consts", "tril")] + 1)
                for sub in range(3):
                    out = side_bank(("mix", g, sub))
                    for x, i in enumerate(part_rows(sub)):
                        n = P if i != SAMPLE else DEC
                        t = mm(out[:, P * x:P * x + n], vn[0:n, g % 2, i, :], wsp_t[0:n, g, 0:n],
                               start=True, stop=True)
                    t.then_inc(side_done, 1)

            def scores(u):
                j, rows = unit_of(u)
                if u == 0:
                    pe.wait_ge(side_freed, N_SIDE)
                if u % 5 == 0:
                    pe.wait_ge(proj_evac, last_block(PROJ.index(("q", j))))
                if u >= 2:
                    pe.wait_ge(exp_done, u - 1)
                for x, i in enumerate(rows):
                    for h in range(2):
                        out, at = ps[:, 2 + 2 * (u % 2) + h, :], x * P
                        hp = slice(DH * h, DH * h + DH)
                        if i == SAMPLE:
                            q = cat[hp, j, SEQ:TOK]
                            mm(out[0:DEC, at:at + DEC], q, k_t[hp, SEQ:TOK], start=True, stop=True)
                            last = mm(out[0:DEC, at + DEC:at + DEC + DH], q, kc_t[hp, :], start=True, stop=True)
                            continue
                        even, odd = P * i, P * i + DH
                        q = cat[hp, j, even:even + DH]
                        mm(out[0:DH, at:at + DH], q, k_t[hp, even:even + DH], start=True, stop=True)
                        if i == 0:
                            mm(out[0:DH, at + DH:at + P], neg_row[:, :], one_row[:, :], start=True, stop=True)
                        else:
                            mm(out[0:DH, at + DH:at + P], q, k_t[hp, even - DH:even], start=True, stop=True)
                        last = mm(out[DH:P, at:at + P], cat[hp, j, odd:odd + DH], k_t[hp, even:even + P],
                                  start=True, stop=True)
                last.then_inc(scores_done, 1)

            def turn_probs(u):
                j, rows = unit_of(u)
                pe.wait_ge(probs_ready, u + 1)
                if u >= 1:
                    pe.wait_ge(probs_t_ready, u)
                for x, i in enumerate(rows):
                    for h in range(2):
                        at = (2 * h + x) * P
                        if i == SAMPLE:
                            t = turn(ps[0:DEC + DH, 6, at:at + DEC], probs[0:DEC, u % 3, 2 * h, 0:DEC + DH],
                                     ident[0:DEC, 0:DEC])
                        else:
                            t = turn(ps[:, 6, at:at + P], probs[:, u % 3, 2 * h + x, :], ident[:, :])
                t.then_inc(probs_turned, 1)

            def probs_v(u):
                j, rows = unit_of(u)
                pe.wait_ge(probs_t_ready, u + 1)
                if u == 0:
                    pe.wait_ge(v_even_zero, 1)
                if u >= 1:
                    pe.wait_ge(attn_ready, u)
                for x, i in enumerate(rows):
                    for h in range(2):
                        hc = slice(DH * h, DH * h + DH)
                        if i == SAMPLE:
                            n = DEC + DH
                            last = mm(ps[hc, 7, 0:DEC], v_sample[0:n, hc], probs_t[0:n, u % 2, 2 * h, 0:DEC],
                                      start=True, stop=True)
                            continue
                        for half, v in enumerate((v_even, v_nat)):
                            at = P * x + DH * half
                            last = mm(ps[hc, 7, at:at + DH], v[:, i, hc],
                                      probs_t[:, u % 2, 2 * h + x, DH * half:DH * half + DH],
                                      start=True, stop=True)
                last.then_inc(pv_done, 1)

            def tick(t):
                if t < UNITS:
                    scores(t)
                if 0 <= t - 2 < UNITS:
                    turn_probs(t - 2)
                if 0 <= t - 3 < UNITS:
                    probs_v(t - 3)

            def out_proj(i):
                if i == 0:
                    pe.wait_ge(proj_evac, N_BLOCKS)
                if i >= 2:
                    pe.wait_ge(y_added, i - 1)
                pe.wait_ge(cat_lo, i + 1)
                if i == SAMPLE:
                    pe.wait_ge(sample_ready, 1)
                for k in range(KT):
                    if i == 0:
                        pe.wait_ge(split_lo, PLACE[UNIT_WOUT + k] + 1)
                    last = row_products(i, k, t_hl, sample_cat, w_hl[:, k, :, :], 2 * (i % 2), k == 0, k == KT - 1)
                last.then_inc(wout_done, 1)

            for item in SCHEDULE:
                kind = item[0]
                if kind == "back":
                    norm_back(item[1])
                elif kind == "block":
                    proj_block(item[1], item[2])
                elif kind == "consts":
                    consts()
                elif kind == "turn":
                    turn_tile(item[1], item[2])
                elif kind == "mix":
                    mix(item[1])
                elif kind == "tick":
                    tick(item[1])
                elif kind == "wout":
                    out_proj(item[1])

            def gate_up(c, s, first):
                f, b = divmod(s, BLOCKS)
                cols = slice(BLK * b, BLK * b + BLK)
                if first:
                    if s < 2:
                        pe.wait_ge(y_added, ROWS - 1 + s)
                        if s == 0:
                            pe.wait_ge(lo_ready, 2 * ROWS - 3)
                    if s == 2:
                        pe.wait_ge(lo_ready, 2 * ROWS)
                if not first or s >= 2:
                    pe.wait_ge(hidden_ready, STEPS * c + (s - 1))
                if b == 0:
                    pe.wait_ge(split_lo, 6 * c + (UNIT_CHUNK + 2 * f))
                for g in range(2):
                    for k in range(KT):
                        w = [gu[f][:, 2 * g + p, P * k:P * k + P] for p in range(2)]
                        last = three_passes(ps[:, gate_bank(s) + g, 0:BLK], w,
                                            (t_hi[:, k, cols], t_lo[:, k, cols]), k == 0, k == KT - 1)
                last.then_inc(gu_done, 1)

            def down(c, i, first):
                b = (row_tokens(i).stop - 1) // BLK
                if i < 2:
                    if not first:
                        pe.wait_ge(y_acc, ROWS * c)
                else:
                    pe.wait_ge(y_acc, ROWS * c + (i - 1))
                if i == SAMPLE:
                    pe.wait_ge(sample_ready, c + 2)
                for f in range(2):
                    if i in (0, 2, 5) or i == 3:
                        pe.wait_ge(act_lo_ready, STEPS * c + (BLOCKS * f + b + 1))
                    if i == 0:
                        pe.wait_ge(split_lo, 6 * c + (UNIT_CHUNK + 3 + f))
                    last = row_products(i, f, act_hl, sample_act, w_dn[:, f, :, :], 4 + 2 * (i % 2), f == 0, f == 1)
                last.then_inc(down_done, 1)

            def chunk(c, first):
                for s in range(STEPS):
                    gate_up(c, s, first)
                    if first and s == 0:
                        norm_back(2 * ROWS - 1)
                for i in range(ROWS):
                    down(c, i, first)

            chunk(0, True)
            with pe.Fori(1, CHUNKS - 1) as c:
                chunk(c, False)
            chunk(CHUNKS - 1, False)

        @block.scalar
        def _(act):
            def norm_front(r):
                i = r % ROWS
                rows = row_parts(i)
                if r < ROWS:
                    act.wait_ge(x_landed[i % 4], 16 * (i // 4 + 1))
                    src = xin[rows, i % 4, :]
                elif r < 2 * ROWS:
                    act.wait_ge(y_added, i + 1)
                    src = y_row(i)
                else:
                    act.wait_ge(y_acc, ROWS * (CHUNKS - 1) + i + 1)
                    src = y_row(i)
                if r == ROWS:
                    act.wait_ge(cat_lo, ROWS)
                if 2 <= r < 2 * ROWS and r != ROWS:
                    act.wait_ge(turned, r - 1)
                if r >= 2 * ROWS:
                    act.wait_ge(gu_done, STEPS * CHUNKS)
                    if i >= OUT_RING:
                        act.wait_ge(y_out[i % OUT_RING], 16)
                dst = xn[rows, i % 2, :] if r < 2 * ROWS else xo[rows, i % OUT_RING, :]
                nc.scalar.activation(dst, src, ACT.Square,
                                     accum_out=sumsq[rows, r:r + 1]).then_inc(sumsq_ready, 1)

            def norm_back(r):
                i = r % ROWS
                n = P if i != SAMPLE else DEC
                act.wait_ge(turned, r + 1)
                nc.scalar.copy(t_hi[:, :, row_tokens(i)], turned_pair(r)[:, :, 0:n]).then_inc(hi_ready, 1)

            def split(n):
                unit_landed(act, n)
                if 2 <= n < N_PROJ:
                    act.wait_ge(proj_done, last_block(n - 2))
                if n == UNIT_WOUT + 6:
                    act.wait_ge(proj_done, last_block(N_PROJ - 2))
                if n == UNIT_WOUT + 7:
                    act.wait_ge(proj_done, last_block(N_PROJ - 1))
                if n == UNIT_FFN:
                    act.wait_ge(cat_lo, ROWS)
                nc.scalar.copy(unit_parts(n)[0], unit_stage(n)).then_inc(split_hi, 1)

            def evacuate(n):
                t, b = PROJ_BLOCKS[n]
                kind, j = PROJ[t]
                cols = slice(BLK * b, BLK * b + BLK)
                act.wait_ge(proj_done, n + 1)
                src = ps[:, proj_bank(n), 0:BLK]
                if kind in "vgu" and b == 0 and trans_user_before(t) is not None:
                    before = trans_user_before(t)
                    bk, bj = PROJ[before]
                    if bk == "u":
                        act.wait_ge(m_ready, BLOCKS * (bj + 1))
                    else:
                        act.wait_ge(side_done, SIDE[("turn", bk, bj, 2)] + 1)
                if kind == "k":
                    out = nc.scalar.copy(k_t[:, cols], src)
                elif kind == "q":
                    out = nc.scalar.copy(cat[:, j, cols], src)
                elif kind == "v" or t == LATE_U:
                    out = nc.scalar.copy(trans[:, t % 2, cols], src)
                else:
                    out = nc.scalar.activation(trans[:, t % 2, cols], src, ACT.Gelu)
                out.then_inc(proj_evac, 1)

            def late_gelu():
                act.wait_ge(proj_evac, last_block(LATE_U))
                nc.scalar.activation(trans[:, LATE_U % 2, :], trans[:, LATE_U % 2, :],
                                     ACT.Gelu).then_inc(late_gelu_done, 1)

            def tick(u):
                if u >= UNITS:
                    return
                j, n, tiles, keys = unit_shape(u)
                if u == 0:
                    for g in range(2):
                        act.wait_ge(g_state_out[g], 32)
                act.wait_ge(sink_in_ready, u + 1)
                if u >= 3:
                    act.wait_ge(probs_turned, u - 2)
                nc.scalar.activation(stat(sink_exp, u), stat(sink_in, u), ACT.Exp)
                for h in range(2):
                    for x in range(tiles):
                        e = nc.scalar.activation(prob(u)[:, h, x, :], score(u)[:, h, x, :], ACT.Exp,
                                                 bias=stat(nmax, u)[:, h, x:x + 1], scale=SCALE,
                                                 accum_out=stat(psums, u)[:, h, x:x + 1])
                e.then_inc(exp_done, 1)

            def split_cat(i):
                b = (row_tokens(i).stop - 1) // BLK
                act.wait_ge(proj_done, N_BLOCKS - BLOCKS + b + 1)
                act.wait_ge(m_ready, GROUPS * BLOCKS - BLOCKS + b + 1)
                act.wait_ge(attn_ready, UNITS - 5 + i // 2 + 1)
                tk = row_tokens(i)
                nc.scalar.copy(t_hi[:, :, tk], cat[:, :, tk]).then_inc(cat_hi, 1)

            for item in SCHEDULE:
                kind = item[0]
                if kind == "front":
                    norm_front(item[1])
                elif kind == "back":
                    norm_back(item[1])
                elif kind == "split":
                    split(item[1])
                elif kind == "evac":
                    evacuate(item[1])
                elif kind == "late":
                    late_gelu()
                elif kind == "tick":
                    tick(item[1])
                elif kind == "cat":
                    split_cat(item[1])
                    if item[1] == SAMPLE:
                        act.wait_ge(cat_lo, ROWS)
                        nc.scalar.copy(sample_cat[:, :, :, :].rearrange("p k h t -> p h k t"),
                                       t_hl[:, :, :, SEQ:TOK]).then_inc(sample_ready, 1)

            def gather_sample(c, first):
                if first:
                    act.wait_ge(wout_done, ROWS)
                else:
                    act.wait_ge(down_done, ROWS * c)
                act.wait_ge(act_lo_ready, STEPS * c + STEPS)
                nc.scalar.copy(sample_act.rearrange("p f h t -> p h f t"),
                               act_hl[:, :, :, SEQ:TOK]).then_inc(sample_ready, 1)

            def step(c, s, first):
                act.wait_ge(gu_done, STEPS * c + (s + 1))
                if not first or s >= 2:
                    act.wait_ge(hidden_ready, STEPS * c + (s - 1))
                nc.scalar.activation(silu[:, s % 2, :], ps[:, gate_bank(s), 0:BLK], ACT.Silu).then_inc(silu_ready, 1)
                act.wait_ge(hidden_ready, STEPS * c + (s + 1))
                f, b = divmod(s, BLOCKS)
                nc.scalar.copy(act_hi[:, f, BLK * b:BLK * b + BLK], hidden[:, s % 2, :]).then_inc(act_hi_ready, 1)

            def split_chunk(c, k):
                n = UNIT_CHUNK + k
                act.wait_ge(stage_landed[n % STAGE], 64 * c + 32 * (n // STAGE + 1))
                if k >= 4:
                    act.wait_ge(gu_done, STEPS * c + BLOCKS)
                nc.scalar.copy(chunk_parts(k)[0], stage[:, n % STAGE, :]).then_inc(split_hi, 1)

            def chunk(c, first, last):
                for s in range(STEPS):
                    step(c, s, first)
                    if first and s == 0:
                        norm_back(2 * ROWS - 1)
                    if s in (0, 1):
                        split_chunk(c, s)
                    if s in (3, 4):
                        split_chunk(c, s - 1)
                gather_sample(c, first)
                if not last:
                    split_chunk(c, 4)
                    split_chunk(c, 5)

            chunk(0, True, False)
            with act.Fori(1, CHUNKS - 1) as c:
                chunk(c, False, False)
            chunk(CHUNKS - 1, False, True)
            for i in range(ROWS):
                norm_front(2 * ROWS + i)

        @block.vector
        def _(dve):
            def low(out, x, hi):
                return nc.vector.tensor_tensor(out, x, hi.bitcast(F32), ALU.subtract)

            nc.vector.memset(v_even[DH:P, 0, :], 0.0).then_inc(v_even_zero, 1)

            def sinks():
                dve.wait_ge(sink_landed, 16)
                by_pair = sink8[:, :].rearrange("p (h j) -> p j h", h=2)
                for x in range(2):
                    nc.vector.tensor_copy(sink[:, :, :, x], by_pair).then_inc(sinks_ready, 1)
                    nc.vector.tensor_scalar(nsink[:, :, :, x], by_pair, -1.0, None, ALU.mult).then_inc(sinks_ready, 1)

            def norm_front(r):
                i = r % ROWS
                rows = row_parts(i)
                src = xin[rows, i % 4, :] if r < ROWS else y_row(i)
                if i == 0:
                    dve.wait_ge(gain_landed, 16 * (r // ROWS + 1))
                dve.wait_ge(rstd_ready, r + 1)
                dst = xn[rows, i % 2, :] if r < 2 * ROWS else xo[rows, i % OUT_RING, :]
                nc.vector.scalar_tensor_tensor(out=dst, in0=src, scalar=rstd[rows, r:r + 1],
                                               in1=gain[rows, :], op0=ALU.mult,
                                               op1=ALU.mult).then_inc(xn_ready, 1)

            def norm_back(r):
                i = r % ROWS
                n = P if i != SAMPLE else DEC
                tk = row_tokens(i)
                dve.wait_ge(hi_ready, r + 1)
                low(t_lo[:, :, tk], turned_pair(r)[:, :, 0:n], t_hi[:, :, tk]).then_inc(lo_ready, 1)

            def split(n):
                dve.wait_ge(split_hi, PLACE[n] + 1)
                hi, lo = unit_parts(n)
                low(lo, unit_stage(n), hi).then_inc(split_lo, 1)

            def side(item):
                m = SIDE[item]
                dve.wait_ge(side_done, m + 1)
                return ps[:, 4 + m % 4, :]

            def consts():
                src = side(("consts", "tril"))
                nc.vector.tensor_copy(wsp_t[:, :, :], src.rearrange("p (g s) -> p g s", g=GROUPS)).then_inc(side_freed, 1)
                src = side(("consts", "cache"))
                nc.vector.tensor_copy(kc_t, src[:, 0:DH]).then_inc(side_freed, 1)

            def turn_tile(kind, g):
                if kind == "k":
                    src = side(("turn", "k", 0, 0))
                    for x in range(2):
                        dve.wait_ge(g_state_out[x], 32)
                    nc.vector.tensor_copy(k_state[:, 0, :], src[:, 0:P]).then_inc(v_copied, 1)
                    nc.vector.tensor_copy(k_state[0:DEC, 1, :], src[0:DEC, P:2 * P]).then_inc(side_freed, 1)
                    return
                if kind == "v":
                    for sub in range(2):
                        src = side(("turn", "v", 0, sub)).rearrange("p (i c) -> p i c", i=4)
                        i0 = 4 * sub
                        nc.vector.tensor_copy(v_nat[:, i0:i0 + 4, :], src).then_inc(v_copied, 1)
                        nc.vector.tensor_copy(v_even[0:DH, i0:i0 + 4, :], src[0:DH, :, :]).then_inc(v_copied, 1)
                        n = 4 - sub
                        nc.vector.tensor_copy(v_even[DH:P, i0 + 1:i0 + 1 + n, :],
                                              src[DH:P, 0:n, :]).then_inc(side_freed, 1)
                    src = side(("turn", "v", 0, 2))
                    nc.vector.tensor_copy(v_sample[0:DEC, :], src[0:DEC, 0:P]).then_inc(side_freed, 1)
                    return
                if g == 0:
                    dve.wait_ge(small_landed, 48)
                    dve.wait_ge(pool_consts, 6)
                if g >= 2:
                    dve.wait_ge(g_state_out[g % 2], 16)
                for sub in range(3):
                    src = side(("turn", "g", g, sub))
                    rows = part_rows(sub)
                    n = P if sub < 2 else DEC
                    for x, i in enumerate(rows):
                        nc.vector.bn_stats(ln_st[0:n, i, :], src[0:n, P * x:P * x + P]).then_inc(ln_stats, 1)
                    for i in rows:
                        dve.wait_ge(ln_stats, ROWS * g + i + 1)
                        nc.vector.bn_aggr(ln_mv[0:n, i, :], ln_st[0:n, i, :]).then_inc(ln_aggr, 1)
                    for x, i in enumerate(rows):
                        dve.wait_ge(ln_aggr, ROWS * g + i + 1)
                        nc.vector.scalar_tensor_tensor(
                            out=vn[0:n, g % 2, i, :], in0=src[0:n, P * x:P * x + P],
                            scalar=ln_mv[0:n, i, 0:1], in1=ln_g[0:n, P * g:P * g + P],
                            op0=ALU.subtract, op1=ALU.mult).then_inc(side_freed if i == rows[-1] else ln_centred, 1)

            def affine(g):
                dve.wait_ge(ln_rstd_ready, g + 1)
                dve.wait_ge(side_freed, SIDE[("turn", "g", g, 2)] + 1)
                for i in range(ROWS):
                    n = P if i != SAMPLE else DEC
                    nc.vector.scalar_tensor_tensor(
                        out=vn[0:n, g % 2, i, :], in0=vn[0:n, g % 2, i, :], scalar=ln_rstd[0:n, i:i + 1],
                        in1=ln_b[0:n, P * g:P * g + P], op0=ALU.mult, op1=ALU.add).then_inc(vn_ready, 1)

            def mix(g):
                for sub in range(3):
                    src = side(("mix", g, sub))
                    if sub < 2:
                        dst = cat[:, PAIRS + g, 512 * sub:512 * sub + 512].rearrange("p (i t) -> p i t", i=4)
                        nc.vector.tensor_tensor(dst, src.rearrange("p (i t) -> p i t", i=4),
                                                bsp[:, g:g + 1, :].to_broadcast([P, 4, P]),
                                                ALU.add).then_inc(side_freed, 1)
                    else:
                        nc.vector.tensor_tensor(cat[:, PAIRS + g, SEQ:TOK], src[:, 0:DEC], bsp[:, g, 0:DEC],
                                                ALU.add).then_inc(side_freed, 1)

            def gate_u(t, b):
                g = PROJ[t][1]
                cols = slice(BLK * b, BLK * b + BLK)
                dve.wait_ge(side_freed, SIDE[("mix", g, 2)] + 1)
                nc.vector.tensor_tensor(cat[:, PAIRS + g, cols], trans[:, t % 2, cols], cat[:, PAIRS + g, cols],
                                        ALU.mult).then_inc(m_ready, 1)

            def evacuated(n):
                t, b = PROJ_BLOCKS[n]
                if PROJ[t][0] == "u" and t != LATE_U:
                    dve.wait_ge(proj_evac, n + 1)
                    gate_u(t, b)

            def late():
                dve.wait_ge(late_gelu_done, 1)
                for b in range(BLOCKS):
                    gate_u(LATE_U, b)

            def maxima(u):
                j, n, tiles, keys = unit_shape(u)
                dve.wait_ge(scores_done, u + 1)
                nc.vector.tensor_reduce(stat(smx, u), score(u), AX_X, ALU.max).then_inc(max_ready, 1)
                dve.wait_ge(max_ready, u + 1)
                if u == 0:
                    dve.wait_ge(sinks_ready, 4)
                nc.vector.scalar_tensor_tensor(out=stat(nmax, u), in0=stat(smx, u), scalar=-SCALE,
                                               in1=nsink[0:n, j, :, 0:tiles], op0=ALU.mult,
                                               op1=ALU.min).then_inc(nmax_ready, 1)
                dve.wait_ge(nmax_ready, u + 1)
                nc.vector.tensor_tensor(stat(sink_in, u), stat(nmax, u), sink[0:n, j, :, 0:tiles],
                                        ALU.add).then_inc(sink_in_ready, 1)

            def normalise(u):
                j, n, tiles, keys = unit_shape(u)
                dve.wait_ge(exp_done, u + 1)
                nc.vector.tensor_tensor(stat(denom, u), stat(psums, u), stat(sink_exp, u),
                                        ALU.add).then_inc(denom_ready, 1)
                dve.wait_ge(denom_ready, u + 1)
                nc.vector.reciprocal(stat(rden, u), stat(denom, u)).then_inc(rden_ready, 1)
                dve.wait_ge(rden_ready, u + 1)
                nc.vector.tensor_tensor(prob(u), prob(u),
                                        stat(rden, u).unsqueeze(3).to_broadcast([n, 2, tiles, keys]),
                                        ALU.mult).then_inc(probs_ready, 1)

            def probs_out(u):
                j, n, tiles, keys = unit_shape(u)
                dve.wait_ge(probs_turned, u + 1)
                src = ps[0:keys, 6, :].rearrange("p (h x c) -> p h x c", h=2, c=P)[:, :, 0:tiles, 0:n]
                dst = probs_t[0:keys, u % 2, :, :].rearrange("p (h x) c -> p h x c", h=2)[:, :, 0:tiles, 0:n]
                nc.vector.tensor_copy(dst, src).then_inc(probs_t_ready, 1)

            def attn_out(u):
                j, rows = unit_of(u)
                dve.wait_ge(pv_done, u + 1)
                t0, t1 = row_tokens(rows[0]).start, row_tokens(rows[-1]).stop
                nc.vector.tensor_copy(cat[:, j, t0:t1], ps[:, 7, 0:t1 - t0]).then_inc(attn_ready, 1)

            def tick(t):
                if t == 0:
                    sinks()
                if t < UNITS:
                    maxima(t)
                if 0 <= t - 1 < UNITS:
                    normalise(t - 1)
                if 0 <= t - 2 < UNITS:
                    probs_out(t - 2)
                if 0 <= t - 3 < UNITS:
                    attn_out(t - 3)

            def split_cat(i):
                tk = row_tokens(i)
                dve.wait_ge(cat_hi, i + 1)
                low(t_lo[:, :, tk], cat[:, :, tk], t_hi[:, :, tk]).then_inc(cat_lo, 1)

            def banks(rows, b):
                return ps[rows, b:b + 2, :].rearrange("p b c -> p (b c)")

            def add_banks(i, b, added):
                nc.vector.tensor_tensor(y_row(i), banks(row_parts(i), b), y_row(i), ALU.add).then_inc(added, 1)

            def sample_low(b, n):
                nc.vector.tensor_tensor(y_row(SAMPLE), banks(slice(DEC, 2 * DEC), b), y_row(SAMPLE),
                                        ALU.add).then_inc(low_added, 1)
                dve.wait_ge(low_added, n)

            def add_out_proj(i):
                dve.wait_ge(wout_done, i + 1)
                dve.wait_ge(y_landed[i], 16)
                if i == SAMPLE:
                    sample_low(2 * (i % 2), 1)
                add_banks(i, 2 * (i % 2), y_added)

            for item in SCHEDULE:
                kind = item[0]
                if kind == "front":
                    norm_front(item[1])
                elif kind == "back":
                    norm_back(item[1])
                elif kind == "split":
                    split(item[1])
                elif kind == "consts":
                    consts()
                elif kind == "turn":
                    turn_tile(item[1], item[2])
                elif kind == "affine":
                    affine(item[1])
                elif kind == "mix":
                    mix(item[1])
                elif kind == "evac":
                    evacuated(item[1])
                elif kind == "late":
                    late()
                elif kind == "tick":
                    tick(item[1])
                elif kind == "cat":
                    split_cat(item[1])
                elif kind == "wout":
                    add_out_proj(item[1])

            def step(c, s, first):
                dve.wait_ge(silu_ready, STEPS * c + (s + 1))
                if not first or s >= 2:
                    dve.wait_ge(act_lo_ready, STEPS * c + (s - 1))
                nc.vector.tensor_tensor(hidden[:, s % 2, :], ps[:, gate_bank(s) + 1, 0:BLK], silu[:, s % 2, :],
                                        ALU.mult).then_inc(hidden_ready, 1)
                f, b = divmod(s, BLOCKS)
                cols = slice(BLK * b, BLK * b + BLK)
                dve.wait_ge(act_hi_ready, STEPS * c + (s + 1))
                low(act_lo[:, f, cols], hidden[:, s % 2, :], act_hi[:, f, cols]).then_inc(act_lo_ready, 1)

            def split_chunk(c, k):
                n = UNIT_CHUNK + k
                dve.wait_ge(split_hi, 6 * c + (n + 1))
                hi, lo = chunk_parts(k)
                low(lo, stage[:, n % STAGE, :], hi).then_inc(split_lo, 1)

            def add_down(c, i):
                dve.wait_ge(down_done, ROWS * c + (i + 1))
                if i == SAMPLE:
                    sample_low(4 + 2 * (i % 2), c + 2)
                add_banks(i, 4 + 2 * (i % 2), y_acc)

            def chunk(c, first, last):
                for s in range(STEPS):
                    step(c, s, first)
                    if first and s == 0:
                        norm_back(2 * ROWS - 1)
                    if s in (0, 1):
                        split_chunk(c, s)
                    if s in (3, 4):
                        split_chunk(c, s - 1)
                for i in range(ROWS):
                    add_down(c, i)
                    if not last and i in (0, 2):
                        split_chunk(c, 4 + i // 2)
                    if last and i >= 1:
                        norm_front(2 * ROWS + i - 1)

            chunk(0, True, False)
            with dve.Fori(1, CHUNKS - 1) as c:
                chunk(c, False, False)
            chunk(CHUNKS - 1, False, True)
            norm_front(3 * ROWS - 1)


_OUTS = [("y_prompt", (1, SEQ, D)), ("y_sample", (1, DEC, D)),
         ("state_attn_k_prompt", (1, 1, P, 2, DH)), ("state_attn_v_prompt", (1, 1, P, 2, DH)),
         ("state_attn_k_sample", (1, 1, P, 2, DH)), ("state_attn_v_sample", (1, 1, P, 2, DH)),
         ("state_gmlp_v_sample", (1, 1, DEC, GROUPS * P))]


def kernel(**inputs):
    import numpy as _np
    import concourse.bacc as _bacc
    from concourse.bass_utils import run_bass_kernel_spmd as _run

    nc = _bacc.Bacc("TRN2", target_bir_lowering=False, num_devices=1, dynamic_dma_scratch_size=1024)
    arrays, ins, outs = {}, {}, {}
    for name, value in inputs.items():
        arr = _np.ascontiguousarray(value)
        arrays[f"in_{name}"] = arr
        ins[name] = nc.dram_tensor(f"in_{name}", arr.shape, mybir.dt.from_np(arr.dtype), kind="ExternalInput").ap()
    for name, shape in _OUTS:
        outs[name] = nc.dram_tensor(f"out_{name}", shape, F32, kind="ExternalOutput").ap()
    build(nc, ins, outs)
    r = _run(nc, [arrays], core_ids=[0])
    return tuple(r.results[0][f"out_{name}"] for name, _ in _OUTS)
```
